# Optimizing a Trainium2 kernel written in Bass

```python
import math
import jax, jax.numpy as jnp
from jax import lax
import numpy as np

D_MODEL = 1024
BATCH = 1
SEQ = 256
DEPTH = 1

CHUNK = 64
N_ATTN_HEADS = 8
HEAD_DIM = 64
ATTN_WIDTH = N_ATTN_HEADS * HEAD_DIM
CONV_GROUPS = 8
CONV_WIDTH_CH = 512
CONV_K = 3
Q_BLOCK = 128
FFN_HIDDEN = int(math.ceil(8 * D_MODEL / 3 / 256) * 256)
RMS_EPS = 1e-6

_COLS = [ATTN_WIDTH, ATTN_WIDTH, ATTN_WIDTH, N_ATTN_HEADS,
         CONV_WIDTH_CH, CONV_WIDTH_CH, CONV_WIDTH_CH,
         D_MODEL, D_MODEL]
IN_COLS = sum(_COLS)
_SPLITS = list(np.cumsum(_COLS)[:-1])


def rmsnorm(x, g):
    xf = x.astype(jnp.float32)
    y = xf * lax.rsqrt(jnp.mean(xf * xf, axis=-1, keepdims=True) + RMS_EPS)
    return (y * g.astype(jnp.float32)).astype(x.dtype)

def causal_depthwise_conv(z, w):
    c = z.shape[-1]
    return lax.conv_general_dilated(
        z, w[:, None, :].astype(z.dtype), window_strides=(1,),
        padding=[(CONV_K - 1, 0)], dimension_numbers=("NWC", "WIO", "NWC"),
        feature_group_count=c)

def forgetting_attention(q, k, v, logf):
    s_len = q.shape[1]
    scale = 1.0 / math.sqrt(q.shape[-1])
    c = jnp.cumsum(logf, axis=1).transpose(0, 2, 1)
    outs = []
    for s0 in range(0, s_len, Q_BLOCK):
        s1 = s0 + Q_BLOCK
        logits = jnp.einsum("bqhd,bkhd->bhqk", q[:, s0:s1], k[:, :s1],
                            preferred_element_type=jnp.float32) * scale
        logits = logits + c[:, :, s0:s1, None] - c[:, :, None, :s1]
        qpos = jnp.arange(s0, s1)[:, None]
        kpos = jnp.arange(s1)[None, :]
        logits = jnp.where(kpos <= qpos, logits, -jnp.inf)
        p = jax.nn.softmax(logits, axis=-1)
        outs.append(jnp.einsum("bhqk,bkhd->bqhd", p.astype(v.dtype), v[:, :s1]))
    return jnp.concatenate(outs, axis=1)

def mixer(h, w_in, b_f, conv_w, w_branch, w_out):
    bsz, s_len, _ = h.shape
    proj = jnp.einsum("bsd,dn->bsn", h, w_in)
    q, k, v, f_logit, g_b, g_c, hc, gate_conv, gate_attn = jnp.split(proj, _SPLITS, axis=-1)
    ya = g_b * causal_depthwise_conv(g_c * hc, conv_w)
    shp = (bsz, s_len, N_ATTN_HEADS, HEAD_DIM)
    logf = jax.nn.log_sigmoid(f_logit.astype(jnp.float32) + b_f.astype(jnp.float32))
    yb = forgetting_attention(q.reshape(shp), k.reshape(shp), v.reshape(shp), logf)
    yb = yb.reshape(bsz, s_len, ATTN_WIDTH)
    ya_d = jnp.einsum("bsc,cd->bsd", ya, w_branch[0])
    yb_d = jnp.einsum("bsc,cd->bsd", yb, w_branch[1])
    merged = jax.nn.sigmoid(gate_conv) * ya_d + jax.nn.sigmoid(gate_attn) * yb_d
    return jnp.einsum("bsd,de->bse", merged, w_out)

def swiglu(h, w_gate_up, w_down):
    gu = jnp.einsum("bsd,df->bsf", h, w_gate_up)
    g, u = jnp.split(gu, 2, axis=-1)
    return jnp.einsum("bsf,fd->bsd", jax.nn.silu(g) * u, w_down)

def first_inputs(seed: int = 0) -> dict:
    key = jax.random.key(seed)
    ks = jax.random.split(key, 12)
    f32 = jnp.float32

    def nrm(k, shape, fan_in):
        return jax.random.normal(k, shape, f32) * (fan_in ** -0.5)

    def gain(k):
        return 1.0 + 0.05 * jax.random.normal(k, (DEPTH, D_MODEL), f32)

    return {
        "x": jax.random.normal(ks[0], (BATCH, SEQ, D_MODEL), f32),
        "norm_mix_pre": gain(ks[1]),
        "norm_mix_post": gain(ks[2]),
        "w_in": nrm(ks[3], (DEPTH, D_MODEL, IN_COLS), D_MODEL),
        "b_f": 2.0 + 0.5 * jax.random.normal(ks[4], (DEPTH, N_ATTN_HEADS), f32),
        "conv_w": nrm(ks[5], (DEPTH, CONV_K, CONV_WIDTH_CH), CONV_K),
        "w_branch": nrm(ks[6], (DEPTH, 2, ATTN_WIDTH, D_MODEL), ATTN_WIDTH),
        "w_out": nrm(ks[7], (DEPTH, D_MODEL, D_MODEL), D_MODEL),
        "norm_ffn_pre": gain(ks[8]),
        "norm_ffn_post": gain(ks[9]),
        "w_gate_up": nrm(ks[10], (DEPTH, D_MODEL, 2 * FFN_HIDDEN), D_MODEL),
        "w_down": nrm(ks[11], (DEPTH, FFN_HIDDEN, D_MODEL), FFN_HIDDEN),
    }

def first_block(x, norm_mix_pre, norm_mix_post, w_in, b_f, conv_w, w_branch, w_out,
              norm_ffn_pre, norm_ffn_post, w_gate_up, w_down):
    for l in range(DEPTH):
        h = rmsnorm(x, norm_mix_pre[l])
        m = mixer(h, w_in[l], b_f[l], conv_w[l], w_branch[l], w_out[l])
        x = x + rmsnorm(m, norm_mix_post[l])
        h = rmsnorm(x, norm_ffn_pre[l])
        f = swiglu(h, w_gate_up[l], w_down[l])
        x = x + rmsnorm(f, norm_ffn_post[l])
    return x


DEPTH_2 = 2

N_MIXERS = 2
N_HEADS = 8
HEAD_DIM_2 = D_MODEL // N_HEADS
DIFF_HALF = HEAD_DIM_2 // 2
MOBA_BLOCK = 256
MOBA_TOPK = 3
D_FF = -(-8 * D_MODEL // (3 * 256)) * 256
N_BUCKETS = 32
MAX_EXACT = N_BUCKETS // 2
MAX_DISTANCE = 2048
N_MOBA_LAYERS = (DEPTH_2 + 1) // 2
N_DIFF_LAYERS = DEPTH_2 // 2
NEG_INF = -1e30


def rms_norm(x, g):
    x32 = x.astype(jnp.float32)
    y = x32 * lax.rsqrt(jnp.mean(x32 * x32, axis=-1, keepdims=True) + RMS_EPS)
    return (y * g.astype(jnp.float32)).astype(x.dtype)

def t5_bucket(rel):
    n = jnp.maximum(rel, 0)
    nf = jnp.maximum(n, 1).astype(jnp.float32)
    large = MAX_EXACT + (jnp.log(nf / MAX_EXACT) / math.log(MAX_DISTANCE / MAX_EXACT)
                         * (N_BUCKETS - MAX_EXACT)).astype(jnp.int32)
    large = jnp.minimum(large, N_BUCKETS - 1)
    return jnp.where(n < MAX_EXACT, n, large)

def moba_attention(h, w_qkv, w_o, rel_table):
    B, S, _ = h.shape
    pad = (-S) % MOBA_BLOCK
    s_pad = S + pad
    nb = s_pad // MOBA_BLOCK
    nq = s_pad // Q_BLOCK
    k_sel_n = min(MOBA_TOPK, nb)
    q, k, v = jnp.split(h @ w_qkv, 3, axis=-1)

    def heads(t):
        t = t.reshape(B, S, N_HEADS, HEAD_DIM_2).transpose(0, 2, 1, 3)
        return jnp.pad(t, ((0, 0), (0, 0), (0, pad), (0, 0)))

    q = heads(q) * (HEAD_DIM_2 ** -0.5)
    k, v = heads(k), heads(v)
    k_blk = k.reshape(B, N_HEADS, nb, MOBA_BLOCK, HEAD_DIM_2)
    v_blk = v.reshape(B, N_HEADS, nb, MOBA_BLOCK, HEAD_DIM_2)
    k_mean = jnp.mean(k_blk, axis=3)
    q_blocks = q.reshape(B, N_HEADS, nq, Q_BLOCK, HEAD_DIM_2).transpose(2, 0, 1, 3, 4)
    b_idx = jnp.arange(B)[:, None, None, None]
    h_idx = jnp.arange(N_HEADS)[None, :, None, None]
    table_t = rel_table.T

    def one_block(args):
        qb, qi = args
        q_pos = qi * Q_BLOCK + jnp.arange(Q_BLOCK)
        own = qi // (MOBA_BLOCK // Q_BLOCK)
        gate = jnp.einsum('bhqd,bhnd->bhqn', qb, k_mean).astype(jnp.float32)
        gate = jnp.where(jnp.arange(nb) < own, gate, NEG_INF)
        _, sel = lax.top_k(gate, k_sel_n)
        slot_valid = jnp.repeat(jnp.arange(k_sel_n) < own, MOBA_BLOCK)
        k_sel = k_blk[b_idx, h_idx, sel].reshape(B, N_HEADS, Q_BLOCK, k_sel_n * MOBA_BLOCK, HEAD_DIM_2)
        v_sel = v_blk[b_idx, h_idx, sel].reshape(B, N_HEADS, Q_BLOCK, k_sel_n * MOBA_BLOCK, HEAD_DIM_2)
        k_pos_sel = (sel[..., None] * MOBA_BLOCK + jnp.arange(MOBA_BLOCK)).reshape(
            B, N_HEADS, Q_BLOCK, k_sel_n * MOBA_BLOCK)
        bias_sel = table_t[h_idx, t5_bucket(q_pos[None, None, :, None] - k_pos_sel)]
        s_sel = jnp.einsum('bhqd,bhqkd->bhqk', qb, k_sel).astype(jnp.float32) + bias_sel.astype(jnp.float32)
        s_sel = jnp.where(slot_valid, s_sel, NEG_INF)
        k_own = lax.dynamic_slice_in_dim(k, own * MOBA_BLOCK, MOBA_BLOCK, axis=2)
        v_own = lax.dynamic_slice_in_dim(v, own * MOBA_BLOCK, MOBA_BLOCK, axis=2)
        k_pos_own = own * MOBA_BLOCK + jnp.arange(MOBA_BLOCK)
        rel_own = q_pos[:, None] - k_pos_own[None, :]
        bias_own = jnp.moveaxis(rel_table[t5_bucket(rel_own)], -1, 0)
        s_own = jnp.einsum('bhqd,bhkd->bhqk', qb, k_own).astype(jnp.float32) + bias_own[None].astype(jnp.float32)
        s_own = jnp.where(rel_own >= 0, s_own, NEG_INF)
        p = jax.nn.softmax(jnp.concatenate([s_sel, s_own], axis=-1), axis=-1).astype(v.dtype)
        n_sel = k_sel_n * MOBA_BLOCK
        return (jnp.einsum('bhqk,bhqkd->bhqd', p[..., :n_sel], v_sel)
                + jnp.einsum('bhqk,bhkd->bhqd', p[..., n_sel:], v_own))

    o = lax.map(one_block, (q_blocks, jnp.arange(nq)))
    o = o.transpose(1, 0, 3, 2, 4).reshape(B, s_pad, D_MODEL)[:, :S]
    return o @ w_o

def diff_attention(h, w_qkv, w_o, lam, subln_g, rel_table, layer_idx):
    B, S, _ = h.shape
    nq = S // Q_BLOCK
    lambda_init = 0.8 - 0.6 * math.exp(-0.3 * layer_idx)
    q, k, v = jnp.split(h @ w_qkv, 3, axis=-1)
    q = q.reshape(B, S, N_HEADS, 2, DIFF_HALF).transpose(0, 2, 3, 1, 4) * (DIFF_HALF ** -0.5)
    k = k.reshape(B, S, N_HEADS, 2, DIFF_HALF).transpose(0, 2, 3, 1, 4)
    v = v.reshape(B, S, N_HEADS, HEAD_DIM_2).transpose(0, 2, 1, 3)
    lam32 = lam.astype(jnp.float32)
    lam_full = (jnp.exp(jnp.sum(lam32[0] * lam32[1])) - jnp.exp(jnp.sum(lam32[2] * lam32[3]))
                + lambda_init)
    q_blocks = q.reshape(B, N_HEADS, 2, nq, Q_BLOCK, DIFF_HALF).transpose(3, 0, 1, 2, 4, 5)
    k_pos = jnp.arange(S)

    def one_block(args):
        qb, qi = args
        q_pos = qi * Q_BLOCK + jnp.arange(Q_BLOCK)
        rel = q_pos[:, None] - k_pos[None, :]
        bias = jnp.moveaxis(rel_table[t5_bucket(rel)], -1, 0)
        s = jnp.einsum('bhcqd,bhckd->bhcqk', qb, k).astype(jnp.float32) + bias[None, :, None].astype(jnp.float32)
        s = jnp.where(rel >= 0, s, NEG_INF)
        p = jax.nn.softmax(s, axis=-1)
        a = p[:, :, 0] - lam_full * p[:, :, 1]
        return jnp.einsum('bhqk,bhkd->bhqd', a.astype(v.dtype), v)

    o = lax.map(one_block, (q_blocks, jnp.arange(nq)))
    o = o.transpose(1, 2, 0, 3, 4).reshape(B, N_HEADS, S, HEAD_DIM_2)
    o = rms_norm(o, subln_g) * (1.0 - lambda_init)
    o = o.transpose(0, 2, 1, 3).reshape(B, S, D_MODEL)
    return o @ w_o

def swiglu_2(h, w_in, w_out):
    g, u = jnp.split(h @ w_in, 2, axis=-1)
    return (jax.nn.silu(g) * u) @ w_out

def second_inputs(seed: int = 0) -> dict:
    key = jax.random.key(seed)
    ks = jax.random.split(key, 16)
    f32 = jnp.float32
    D = D_MODEL
    return {
        "x": jax.random.normal(ks[0], (BATCH, SEQ, D), f32),
        "c": jax.random.normal(ks[1], (BATCH, D), f32),
        "rel_bias": 0.5 * jax.random.normal(ks[2], (N_BUCKETS, N_HEADS), f32),
        "ada_w": jax.random.normal(ks[3], (DEPTH_2, D, 6 * D), f32) * D ** -0.5,
        "ada_b": 0.01 * jax.random.normal(ks[4], (DEPTH_2, 6 * D), f32),
        "norm_g": 1.0 + 0.1 * jax.random.normal(ks[5], (DEPTH_2, 4, D), f32),
        "moba_w_qkv": jax.random.normal(ks[6], (N_MOBA_LAYERS, D, 3 * D), f32) * D ** -0.5,
        "moba_w_o": jax.random.normal(ks[7], (N_MOBA_LAYERS, D, D), f32) * D ** -0.5,
        "diff_w_qkv": jax.random.normal(ks[8], (N_DIFF_LAYERS, D, 3 * D), f32) * D ** -0.5,
        "diff_w_o": jax.random.normal(ks[9], (N_DIFF_LAYERS, D, D), f32) * D ** -0.5,
        "diff_lambda": 0.1 * jax.random.normal(ks[10], (N_DIFF_LAYERS, 4, DIFF_HALF), f32),
        "diff_subln_g": 1.0 + 0.1 * jax.random.normal(ks[11], (N_DIFF_LAYERS, HEAD_DIM_2), f32),
        "ffn_w_in": jax.random.normal(ks[12], (DEPTH_2, D, 2 * D_FF), f32) * D ** -0.5,
        "ffn_w_out": jax.random.normal(ks[13], (DEPTH_2, D_FF, D), f32) * D_FF ** -0.5,
    }

def second_block(x, c, rel_bias, ada_w, ada_b, norm_g, moba_w_qkv, moba_w_o, diff_w_qkv, diff_w_o,
              diff_lambda, diff_subln_g, ffn_w_in, ffn_w_out):
    c_act = jax.nn.silu(c)
    for i in range(DEPTH_2):
        mod = (c_act @ ada_w[i] + ada_b[i])[:, None, :]
        sh_a, sc_a, g_a, sh_f, sc_f, g_f = jnp.split(mod, 6, axis=-1)
        h = rms_norm(x, norm_g[i, 0]) * (1.0 + sc_a) + sh_a
        if i % N_MIXERS == 0:
            y = moba_attention(h, moba_w_qkv[i // 2], moba_w_o[i // 2], rel_bias)
        else:
            y = diff_attention(h, diff_w_qkv[i // 2], diff_w_o[i // 2], diff_lambda[i // 2],
                               diff_subln_g[i // 2], rel_bias, i)
        x = x + g_a * rms_norm(y, norm_g[i, 1])
        h = rms_norm(x, norm_g[i, 2]) * (1.0 + sc_f) + sh_f
        x = x + g_f * rms_norm(swiglu_2(h, ffn_w_in[i], ffn_w_out[i]), norm_g[i, 3])
    return x


def setup_inputs(seed=0):
    out = dict(first_inputs(seed))
    for name, value in second_inputs(seed + 1).items():
        if name != "x":
            out[name + "_2"] = value
    return out


def reference(
    x, norm_mix_pre, norm_mix_post, w_in, b_f, conv_w, w_branch, w_out, norm_ffn_pre,
    norm_ffn_post, w_gate_up, w_down, c_2, rel_bias_2, ada_w_2, ada_b_2, norm_g_2, moba_w_qkv_2,
    moba_w_o_2, diff_w_qkv_2, diff_w_o_2, diff_lambda_2, diff_subln_g_2, ffn_w_in_2,
    ffn_w_out_2,
):
    x = first_block(
        x, norm_mix_pre, norm_mix_post, w_in, b_f, conv_w, w_branch, w_out, norm_ffn_pre,
        norm_ffn_post, w_gate_up, w_down,
    )
    return second_block(
        x, c_2, rel_bias_2, ada_w_2, ada_b_2, norm_g_2, moba_w_qkv_2, moba_w_o_2, diff_w_qkv_2,
        diff_w_o_2, diff_lambda_2, diff_subln_g_2, ffn_w_in_2, ffn_w_out_2,
    )


_drawn_inputs = setup_inputs


def setup_inputs(seed=0):
    import zlib

    import numpy as np

    out = dict(_drawn_inputs(seed))
    spreads = {}
    factors = {'ada_b_2': 3.645}
    for name, (base, spread) in spreads.items():
        noise = np.random.default_rng([zlib.crc32(name.encode()), seed]).standard_normal(out[name].shape)
        drawn = base * np.exp(spread * noise) if base else spread * noise
        out[name] = __import__('jax').numpy.asarray(drawn.astype(out[name].dtype))
    for name, factor in factors.items():
        out[name] = (out[name] * factor).astype(out[name].dtype)
    return out
```

```python
import math
from contextlib import ExitStack
from functools import partial

import concourse.bass as bass
from concourse import mybir

F32 = mybir.dt.float32
F32R = mybir.dt.float32r
ALU = mybir.AluOpType
ACT = mybir.ActivationFunctionType
AX_X = mybir.AxisListType.X

P = 128
S = 256
NT = S // P
D = 1024
KC = D // P
H = 8
HD1 = 64
AW = H * HD1
AC = AW // P
HD2 = D // H
DIFF = HD2 // 2
FF = -(-8 * D // (3 * 256)) * 256
FG = FF // 256
BUCKETS = 32
EPS = 1e-6
NEG = -1e30
LAMBDA_INIT = 0.8 - 0.6 * math.exp(-0.3 * 1)

SLAB = 2048
N_RAW, N_HI, N_LO = 6, 4, 4
AHEAD = 3

COLUMNS = {}
for _name, _n in (("mix_pre", KC), ("ffn_pre", KC), ("c", KC), ("g00", KC), ("g02", KC), ("g10", KC), ("g12", KC),
                  ("conv", 3 * AC), ("subln", 1), ("b_f", NT * H), ("lam", 4 * DIFF)):
    COLUMNS[_name] = (sum(w for _, w in COLUMNS.values()), _n)
N_COLUMNS = sum(w for _, w in COLUMNS.values())

IDENT, ONES, FLIP, TRI = 0, P, 2 * P, 3 * P
MASK = TRI + NT * S
N_CONST = MASK + S
BIAS_W = 3 * P


class Mark:

    def __init__(self, sem, value):
        self.sem, self.value = sem, value


class Counter:

    def __init__(self, sem):
        self.sem, self.count = sem, 0

    def step(self, n):
        self.count += n
        return Mark(self.sem, self.count)


class Queue:

    def __init__(self, counter):
        self.counter, self.items, self.seen = counter, [], {}

    def wait(self, *marks):
        for m in marks:
            if m is not None and self.seen.get(id(m.sem), 0) < m.value:
                self.seen[id(m.sem)] = m.value
                self.items.append((None, m.sem, m.value))

    def do(self, issue):
        self.items.append((issue, None, 0))

    def step(self, issue):
        m = self.counter.step(1)
        self.items.append((issue, m.sem, 1))
        return m

    def dma(self, issue, counter):
        m = counter.step(16)
        self.items.append((issue, m.sem, 16))
        return m

    def play(self, engine):
        for issue, sem, n in self.items:
            if issue is None:
                engine.wait_ge(sem, n)
            elif sem is None:
                issue()
            else:
                issue().then_inc(sem, n)


def slab_order():
    def ffn(gate_up, down, base):
        order = []
        for g in range(FG):
            order += [(gate_up, base * 2 * FG + g), (gate_up, base * 2 * FG + FG + g)]
            if g:
                order.append((down, base * FG + g - 1))
        return order + [(down, base * FG + FG - 1)]

    order = [("v1", 0), ("v1", 1)]
    for i in range(2):
        order += [("qk1", i), ("qk1", 2 + i)]
    order += [("mix", 2), ("mix", 4), ("mix", 3), ("mix", 5), ("mix", 0), ("mix", 1)]
    order += [("mix", 6 + i) for i in range(8)]
    order += [("branch", i) for i in range(4)] + [("out1", i) for i in (0, 2, 1, 3)]
    order += ffn("gate_up1", "down1", 0)
    for i, name in enumerate(("moba", "diff")):
        order += [(name + "_v", j) for j in range(4)]
        for j in range(4):
            order += [(name + "_qk", j), (name + "_qk", 4 + j)]
        order += [(name + "_o", j) for j in (0, 2, 1, 3)]
        order += ffn("gate_up2", "down2", i)
    return order


def build_program(nc, dram, out):
    with ExitStack() as ctx:
        def sb(name, shape, dt=F32):
            return ctx.enter_context(nc.sbuf_tensor(name, shape, dt))

        def sem(name):
            return ctx.enter_context(nc.semaphore(name))

        raw = [sb(f"raw{i}", [P, SLAB]) for i in range(N_RAW)]
        high = [sb(f"high{i}", [P, SLAB], F32R) for i in range(N_HI)]
        low = [sb(f"low{i}", [P, SLAB], F32R) for i in range(N_LO)]
        x_res = sb("x_res", [P, NT, D])
        h_hi = sb("h_hi", [P, KC, S], F32R)
        h_lo = sb("h_lo", [P, KC, S], F32R)
        y_hi = sb("y_hi", [P, KC, S], F32R)
        y_lo = sb("y_lo", [P, KC, S], F32R)
        work_a = sb("work_a", [P, NT * D])
        work_b = sb("work_b", [P, KC, S])
        work_v = sb("work_v", [P, NT, D])
        bias = sb("bias", [P, H, S])
        gain = [sb(f"gain{i}", [P, D]) for i in range(3)]
        ada = sb("ada", [P, SLAB])
        prob = [sb(f"prob{i}", [P, 3 * P]) for i in range(4)]
        prob_t = [sb(f"prob_t{i}", [P, 3 * P]) for i in range(2)]
        const = sb("const", [P, N_CONST])
        cols = sb("cols", [P, N_COLUMNS])
        c_act = sb("c_act", [P, KC])
        mod_cols = sb("mod_cols", [P, 8, KC])
        stat = sb("stat", [P, 32])
        soft = sb("soft", [P, 4, 8])
        lam_sb = sb("lam_sb", [P, 4])
        lam_pr = sb("lam_pr", [P, 2 * DIFF])
        subln_sc = sb("subln_sc", [P, 1])
        wf_raw = sb("wf_raw", [P, KC * H])
        wf_hi = sb("wf_hi", [P, KC * H], F32R)
        wf_lo = sb("wf_lo", [P, KC * H], F32R)
        gate_f = sb("gate_f", [P, 5, NT * H])
        c_q = sb("c_q", [P, NT * H])
        diff_stat = sb("diff_stat", [P, 2, NT * H])
        psum = [ctx.enter_context(nc.psum_tensor(f"psum{i}", [P, 512], F32)) for i in range(8)]
        bias_dram = nc.dram_tensor("bias_dram", (H, BIAS_W), F32, kind="Internal").ap()

        pe = Queue(Counter(sem("pe_done")))
        act = Queue(Counter(sem("act_done")))
        dve = Queue(Counter(sem("dve_done")))
        pool = Queue(Counter(sem("pool_done")))
        sync = Queue(None)
        raw_in = [Counter(sem(f"raw_in{i}")) for i in range(N_RAW)]
        x_in, const_in, cols_in, wf_in = (Counter(sem(n)) for n in ("x_in", "const_in", "cols_in", "wf_in"))
        bias_sig = Counter(sem("bias_sig"))
        table_in = Counter(sem("table_in"))
        ada_in = Counter(sem("ada_in"))
        gain_in = [Counter(sem(f"gain_in{i}")) for i in range(3)]
        stored = Counter(sem("stored"))

        ident = const[:, IDENT:IDENT + P]
        ones = const[:, ONES:ONES + P]
        flip = const[:, FLIP:FLIP + P]
        tri = [const[:, TRI + c * S:TRI + (c + 1) * S] for c in range(NT)]
        mask = const[:, MASK:MASK + S]

        def col(name, a=0, n=None):
            o, w = COLUMNS[name]
            return cols[:, o + a:o + a + (w if n is None else n)]

        x_loaded = sync.dma(partial(nc.sync.dma_start, x_res[:, :, :], dram["x"].rearrange("(t p) d -> p t d", p=P)), x_in)
        cols_loaded = act.dma(partial(nc.scalar.dma_start, cols[:, :], dram["cols"]), cols_in)
        const_loaded = act.dma(partial(nc.scalar.dma_start, const[:, :], dram["const"]), const_in)
        wf_loaded = act.dma(partial(nc.scalar.dma_start, wf_raw[:, :], dram["wf"]), wf_in)

        bank_free = [[] for _ in range(8)]
        turn = [0]

        def take_bank():
            i = turn[0] % 4
            turn[0] += 1
            pe.wait(*bank_free[i])
            bank_free[i] = []
            return i

        main = slab_order()
        stream = []
        n_ada = 0
        for m, key in enumerate(main):
            stream.append(("main", m))
            if m % 2 == 1 and n_ada < 48:
                stream.append(("ada", n_ada))
                n_ada += 1
        raw_free = [None] * N_RAW
        loads = [0]
        raw_loaded = {}

        def load_next():
            i = loads[0]
            if i >= len(stream):
                return
            loads[0] += 1
            kind, n = stream[i]
            src = dram["ada"][n] if kind == "ada" else dram[main[n][0]][main[n][1]]
            slot = i % N_RAW
            sync.wait(raw_free[slot])
            raw_loaded[i] = sync.dma(partial(nc.sync.dma_start, raw[slot][:, :], src), raw_in[slot])

        slab_used = {}
        slab_split = {}
        done_items = [0]
        pending = []
        ada_state = {"init": None, "free": None}

        def split_next():
            i = done_items[0]
            done_items[0] += 1
            kind, n = stream[i]
            slot = i % N_RAW
            src = raw[slot]
            if kind == "main":
                hi, lo = high[n % N_HI], low[n % N_LO]
                act.wait(raw_loaded[i], slab_used.get(n - N_HI))
                rounded = act.step(partial(nc.scalar.activation, hi[:, :], src[:, :], ACT.Copy))
                dve.wait(rounded, slab_used.get(n - N_LO))
                rest = dve.step(partial(nc.vector.tensor_tensor, lo[:, :], src[:, :], hi[:, :].bitcast(F32), ALU.subtract))
                slab_split[n] = (rounded, rest)
                raw_free[slot] = rest
            else:
                block, k = divmod(n, KC)
                if k == 0:
                    pool.wait(ada_state["free"])
                    cleared = pool.step(partial(nc.gpsimd.memset, ada[:, :], 0.0))
                    pool.wait(cleared)
                    ada_state["init"] = pool.dma(partial(nc.gpsimd.dma_start, ada[0:1, :], dram["ada_b"][block:block + 1, :]), ada_in)
                dve.wait(raw_loaded[i], ada_state["init"], c_ready)
                summed = dve.step(partial(nc.vector.scalar_tensor_tensor, 
                    out=ada[:, :], in0=src[:, :], scalar=c_act[:, k:k + 1], in1=ada[:, :], op0=ALU.mult, op1=ALU.add))
                ada_state["init"] = summed
                raw_free[slot] = summed
                if k == KC - 1:
                    pending.append(lambda: finish_ada(block, summed))
            load_next()

        used = [0]

        def next_slab(name, index):
            n = used[0]
            used[0] += 1
            assert main[n] == (name, index), (main[n], name, index)
            while (n + AHEAD not in slab_split) and done_items[0] < len(stream):
                split_next()
            pe.wait(*slab_split[n])
            return n, high[n % N_HI], low[n % N_LO]

        def slab_done(n, mark):
            slab_used[n] = mark
            while pending:
                pending.pop(0)()

        def weights_still(name, index, hi, lo, ready, kcs, n_chunks):
            n, wh, wl = next_slab(name, index)
            wh = wh[:, :].rearrange("p (k n) -> p k n", k=kcs)
            wl = wl[:, :].rearrange("p (k n) -> p k n", k=kcs)
            banks = []
            for j in range(n_chunks):
                if j % 2 == 0:
                    banks.append(take_bank())
                o = psum[banks[-1]][:, (j % 2) * S:(j % 2 + 1) * S]
                for k in range(kcs):
                    pe.wait(*ready(k))
                    a, b = wh[:, k, j * P:(j + 1) * P], wl[:, k, j * P:(j + 1) * P]
                    first, last = k == 0, k == kcs - 1
                    pe.do(partial(nc.tensor.matmul, o, a, hi(k), start=first, stop=False))
                    pe.do(partial(nc.tensor.matmul, o, a, lo(k), start=False, stop=False))
                    issue = partial(nc.tensor.matmul, o, b, hi(k), start=False, stop=last)
                    if last and (j % 2 == 1 or j == n_chunks - 1):
                        mark = pe.step(issue)
                    else:
                        pe.do(issue)
            slab_done(n, mark)
            return banks, mark

        def weights_moving(name, index, hi, lo, ready, kcs, width, bank_of, k0, k_all):
            n, wh, wl = next_slab(name, index)
            wh = wh[:, :].rearrange("p (k n) -> p k n", k=kcs)
            wl = wl[:, :].rearrange("p (k n) -> p k n", k=kcs)
            marks = []
            for t in range(NT):
                for c in range(width // 512):
                    o = psum[bank_of(t, c)]
                    for k in range(kcs):
                        pe.wait(*ready(k0 + k))
                        a, b = hi(k0 + k, t), lo(k0 + k, t)
                        vh, vl = wh[:, k, c * 512:(c + 1) * 512], wl[:, k, c * 512:(c + 1) * 512]
                        first, last = k0 + k == 0, k0 + k == k_all - 1
                        if first:
                            pe.wait(*bank_free[bank_of(t, c)])
                            bank_free[bank_of(t, c)] = []
                        pe.do(partial(nc.tensor.matmul, o[:, :], a, vh, start=first, stop=False))
                        pe.do(partial(nc.tensor.matmul, o[:, :], a, vl, start=False, stop=False))
                        issue = partial(nc.tensor.matmul, o[:, :], b, vh, start=False, stop=last)
                        if k == kcs - 1:
                            marks.append(pe.step(issue))
                        else:
                            pe.do(issue)
            slab_done(n, marks[-1])
            return marks

        gain_ready = [None] * 3
        gain_used = [None] * 3

        def load_gain(slot, src):
            pool.wait(gain_used[slot])
            gain_used[slot] = None
            gain_ready[slot] = pool.dma(partial(nc.gpsimd.dma_start, gain[slot][:, :], src.partition_broadcast(P)), gain_in[slot])

        gain_slot = {(0, 0): 2, (0, 1): 0, (1, 0): 1, (1, 1): 2}
        mod_ready = {}

        def finish_ada(block, summed):
            layer, b = divmod(block, 3)
            last = None
            pe.wait(summed)
            for half in range(2):
                section = 2 * b + half
                part, what = divmod(section, 3)
                if what < 2:
                    i = take_bank()
                    for k in range(KC):
                        a = ada[:, half * D + k * P:half * D + (k + 1) * P]
                        issue = partial(nc.tensor.matmul, psum[i][:, k:k + 1], a, ones[:, 0:1], start=True, stop=True)
                        last = pe.step(issue) if k == KC - 1 else pe.do(issue)
                    dve.wait(last)
                    place = mod_cols[:, 4 * layer + 2 * part + (1 - what), :]
                    if what == 0:
                        got = dve.step(partial(nc.vector.tensor_copy, place, psum[i][:, 0:KC]))
                    else:
                        g = col(f"g{layer}{2 * part}")
                        got = dve.step(partial(nc.vector.scalar_tensor_tensor, 
                            out=place, in0=psum[i][:, 0:KC], scalar=1.0, in1=g, op0=ALU.add, op1=ALU.mult))
                    bank_free[i] = [got]
                    mod_ready[layer, part, what] = got
                else:
                    slot = gain_slot[layer, part]
                    assert gain_used[slot] is None and gain_ready[slot] is not None
                    for c in range(2):
                        i = take_bank()
                        a = ada[:, half * D + c * 512:half * D + (c + 1) * 512]
                        last = pe.step(partial(nc.tensor.matmul, psum[i][:, :], ones, a, start=True, stop=True))
                        dve.wait(last, gain_ready[slot])
                        g = gain[slot][:, c * 512:(c + 1) * 512]
                        got = dve.step(partial(nc.vector.tensor_tensor, g, psum[i][:, :], g, ALU.mult))
                        bank_free[i] = [got]
                    gain_ready[slot] = got
            ada_state["free"] = last

        def inverse_rms(sums, width, n, given):
            dve.wait(*given)
            a = dve.step(partial(nc.vector.tensor_scalar, sums, sums, 1.0 / width, EPS, ALU.mult, ALU.add))
            act.wait(a)
            b = act.step(partial(nc.scalar.activation, sums, sums, ACT.Sqrt))
            dve.wait(b)
            return dve.step(partial(nc.vector.reciprocal, sums, sums))

        h_used = [None]

        def pre_norm(x_ready, scale, shift, given):
            squares = []
            for t in range(NT):
                act.wait(x_ready[t], work_a_used[0])
                squares.append(act.step(partial(nc.scalar.activation, 
                    work_a[:, t * D:(t + 1) * D], x_res[:, t, :], ACT.Square, accum_out=stat[:, t:t + 1])))
            r = inverse_rms(stat[:, 0:NT], D, NT, squares)
            dve.wait(r)
            normed = [dve.step(partial(nc.vector.tensor_scalar, 
                work_a[:, t * D:(t + 1) * D], x_res[:, t, :], stat[:, t:t + 1], None, ALU.mult)) for t in range(NT)]
            ready = []
            pe.wait(const_loaded)
            for b in range(KC // 2):
                i = take_bank()
                for kk in range(2):
                    k = 2 * b + kk
                    for t in range(NT):
                        pe.wait(normed[t])
                        a = work_a[:, t * D + k * P:t * D + (k + 1) * P]
                        o = psum[i][:, kk * S + t * P:kk * S + (t + 1) * P]
                        issue = partial(nc.tensor.transpose, o, a, ident)
                        turned = pe.step(issue) if kk * NT + t == 2 * NT - 1 else pe.do(issue)
                dve.wait(turned, *given)
                for kk in range(2):
                    k = 2 * b + kk
                    o = psum[i][:, kk * S:(kk + 1) * S]
                    if shift is None:
                        full = dve.step(partial(nc.vector.tensor_scalar, 
                            work_b[:, k, :], o, scale[:, k:k + 1], None, ALU.mult))
                    else:
                        full = dve.step(partial(nc.vector.tensor_scalar, 
                            work_b[:, k, :], o, scale[:, k:k + 1], shift[:, k:k + 1], ALU.mult, ALU.add))
                bank_free[i] = [full]
                act.wait(full, h_used[0])
                two = slice(2 * b, 2 * b + 2)
                hi = act.step(partial(nc.scalar.activation, h_hi[:, two, :], work_b[:, two, :], ACT.Copy))
                dve.wait(hi, full)
                lo = dve.step(partial(nc.vector.tensor_tensor, 
                    h_lo[:, two, :], work_b[:, two, :], h_hi[:, two, :].bitcast(F32), ALU.subtract))
                ready += [(hi, lo)] * 2
            work_a_used[0] = turned
            return lambda k: ready[k]

        work_a_used = [None]

        def post_norm(marks, slot):
            squares = []
            for t in range(NT):
                for c in range(2):
                    act.wait(marks[t][c], work_a_used[0])
                    squares.append(act.step(partial(nc.scalar.activation, 
                        work_a[:, (2 * t + c) * 512:(2 * t + c + 1) * 512], psum[4 + 2 * t + c][:, :], ACT.Square,
                        accum_out=stat[:, 4 + 2 * c + t:5 + 2 * c + t])))
            dve.wait(*squares)
            both = dve.step(partial(nc.vector.tensor_tensor, stat[:, 4:6], stat[:, 4:6], stat[:, 6:8], ALU.add))
            r = inverse_rms(stat[:, 4:6], D, NT, [both])
            dve.wait(r, gain_ready[slot])
            result = []
            for t in range(NT):
                for c in range(2):
                    scaled = dve.step(partial(nc.vector.scalar_tensor_tensor, 
                        out=work_a[:, (2 * t + c) * 512:(2 * t + c + 1) * 512], in0=psum[4 + 2 * t + c][:, :],
                        scalar=stat[:, 4 + t:5 + t], in1=gain[slot][:, c * 512:(c + 1) * 512], op0=ALU.mult, op1=ALU.mult))
                    bank_free[4 + 2 * t + c] = [scaled]
                dve.wait(scaled)
                result.append(dve.step(partial(nc.vector.tensor_tensor, 
                    x_res[:, t, :], x_res[:, t, :], work_a[:, t * D:(t + 1) * D], ALU.add)))
            gain_used[slot] = result[-1]
            gain_ready[slot] = None
            work_a_used[0] = result[-1]
            return result

        h_of = (lambda k: h_hi[:, k, :], lambda k: h_lo[:, k, :])
        h_tok = (lambda k, t: h_hi[:, k, t * P:(t + 1) * P], lambda k, t: h_lo[:, k, t * P:(t + 1) * P])
        y_tok = (lambda k, t: y_hi[:, k, t * P:(t + 1) * P], lambda k, t: y_lo[:, k, t * P:(t + 1) * P])

        y_used = [None]
        work_v_used = [None]

        def feed_forward(gate_up, down, base, ready):
            hidden_ready, hidden_used = {}, {}

            def down_group(g):
                s = 2 * (g % 4)
                hi = lambda k, t: y_hi[:, s + k % 2, t * P:(t + 1) * P]
                lo = lambda k, t: y_lo[:, s + k % 2, t * P:(t + 1) * P]
                m = weights_moving(down, base * FG + g, hi, lo, lambda k: hidden_ready[g], 2, D,
                                   lambda t, c: 4 + 2 * t + c, 2 * g, 2 * FG)
                hidden_used[g] = m[-1]
                return m

            for g in range(FG):
                (gate,), gate_done = weights_still(gate_up, base * 2 * FG + g, *h_of, ready, KC, 2)
                s = slice(2 * (g % 4), 2 * (g % 4) + 2)
                tmp = work_v[:, g % 2, :].rearrange("p (a k n) -> p a k n", a=2, k=2)
                pair = lambda i: psum[i][:, :].rearrange("p (k n) -> p k n", k=2)
                act.wait(gate_done, work_v_used[0])
                silu = act.step(partial(nc.scalar.activation, tmp[:, 0], pair(gate), ACT.Silu))
                bank_free[gate] = [silu]
                (up,), up_done = weights_still(gate_up, base * 2 * FG + FG + g, *h_of, ready, KC, 2)
                dve.wait(silu, up_done)
                full = dve.step(partial(nc.vector.tensor_tensor, tmp[:, 1], pair(up), tmp[:, 0], ALU.mult))
                bank_free[up] = [full]
                act.wait(full, hidden_used.get(g - 4), y_used[0])
                hi = act.step(partial(nc.scalar.activation, y_hi[:, s, :], tmp[:, 1], ACT.Copy))
                dve.wait(hi, full)
                lo = dve.step(partial(nc.vector.tensor_tensor, 
                    y_lo[:, s, :], tmp[:, 1], y_hi[:, s, :].bitcast(F32), ALU.subtract))
                hidden_ready[g] = (hi, lo)
                if g:
                    down_group(g - 1)
            h_used[0] = up_done
            m = down_group(FG - 1)
            y_used[0] = m[-1]
            work_v_used[0] = lo
            return [m[0:2], m[2:4]]

        prob_turn, prob_t_turn = [0], [0]
        prob_free, prob_t_free = [None] * 4, [None] * 2
        W0, W1 = slice(0, P), slice(P, 3 * P)

        def softmax(i, score_done, add):
            b = prob_turn[0] % 4
            prob_turn[0] += 1
            z, s = prob[b], soft[:, b, :]
            dve.wait(score_done, prob_free[b])
            for t, w in enumerate((W0, W1)):
                last = dve.step(add(z[:, w], psum[i][:, w], t))
            bank_free[i] = [last]
            dve.wait(last)
            for t, w in enumerate((W0, W1)):
                top = dve.step(partial(nc.vector.tensor_reduce, s[:, t:t + 1], z[:, w], AX_X, ALU.max, negate=True))
            act.wait(top)
            for t, w in enumerate((W0, W1)):
                ex = act.step(partial(nc.scalar.activation, 
                    z[:, w], z[:, w], ACT.Exp, bias=s[:, t:t + 1], accum_out=s[:, 2 + t:3 + t]))
            dve.wait(ex)
            inv = dve.step(partial(nc.vector.reciprocal, s[:, 4:6], s[:, 2:4]))
            return b, inv

        def scale_prob(b, inv):
            z, s = prob[b], soft[:, b, :]
            dve.wait(inv)
            for t, w in enumerate((W0, W1)):
                last = dve.step(partial(nc.vector.tensor_scalar, z[:, w], z[:, w], s[:, 4 + t:5 + t], None, ALU.mult))
            return last

        def turn_prob(b, ready):
            z = prob[b]
            i = take_bank()
            pe.wait(ready)
            for c in range(3):
                issue = partial(nc.tensor.transpose, psum[i][:, c * P:(c + 1) * P], z[:, c * P:(c + 1) * P], ident)
                turned = pe.step(issue) if c == 2 else pe.do(issue)
            prob_free[b] = turned
            u = prob_t_turn[0] % 2
            prob_t_turn[0] += 1
            act.wait(turned, prob_t_free[u])
            copied = act.step(partial(nc.scalar.activation, prob_t[u][:, :], psum[i][:, 0:3 * P], ACT.Copy))
            bank_free[i] = [copied]
            return u, copied

        def scores(q, k, more=None):
            i = take_bank()
            for t, w in enumerate((W0, W1)):
                o = psum[i][:, w]
                issue = partial(nc.tensor.matmul, 
                    o, q[:, t * P:(t + 1) * P], k[:, 0:(t + 1) * P], start=True, stop=more is None)
                if more is None:
                    m = pe.step(issue)
                else:
                    pe.do(issue)
                    m = more(i, t)
            return i, m

        def token_values(name, blocks, ready, width):
            done = []
            for c in range(blocks):
                for half in range(2):
                    m = weights_moving(name, 2 * c + half, *h_tok, ready, KC // 2, 512,
                                       lambda t, _: 4 + 2 * t + c, half * KC // 2, KC)
                for t in range(NT):
                    act.wait(m[t], work_v_used[0])
                    i = 4 + 2 * t + c
                    done.append(act.step(partial(nc.scalar.activation, 
                        work_v[:, t, c * 512:(c + 1) * 512], psum[i][:, :], ACT.Copy)))
                    bank_free[i] = [done[-1]]
            return done

        act.wait(cols_loaded)
        c_ready = act.step(partial(nc.scalar.activation, c_act[:, :], col("c"), ACT.Silu))
        load_gain(0, dram["mix_post"][0])
        load_gain(1, dram["ffn_post"][0])
        load_gain(2, dram["norm_g"][0, 1])
        for _ in range(N_RAW):
            load_next()

        ready = pre_norm([x_loaded] * NT, col("mix_pre"), None, [cols_loaded])
        values_done = token_values("v1", 1, ready, AW)

        act.wait(wf_loaded)
        wf_rounded = act.step(partial(nc.scalar.activation, wf_hi[:, :], wf_raw[:, :], ACT.Copy))
        dve.wait(wf_rounded)
        wf_rest = dve.step(partial(nc.vector.tensor_tensor, wf_lo[:, :], wf_raw[:, :], wf_hi[:, :].bitcast(F32), ALU.subtract))
        fb = take_bank()
        pe.wait(wf_rest)
        for t in range(NT):
            o = psum[fb][:, t * H:(t + 1) * H]
            for k in range(KC):
                a, b = h_tok[0](k, t), h_tok[1](k, t)
                vh, vl = wf_hi[:, k * H:(k + 1) * H], wf_lo[:, k * H:(k + 1) * H]
                pe.do(partial(nc.tensor.matmul, o, a, vh, start=k == 0, stop=False))
                pe.do(partial(nc.tensor.matmul, o, a, vl, start=False, stop=False))
                f_done = pe.step(partial(nc.tensor.matmul, o, b, vh, start=False, stop=k == KC - 1))
        u, a, l, logf, nlogf = (gate_f[:, i, :] for i in range(5))
        dve.wait(f_done, cols_loaded)
        m = dve.step(partial(nc.vector.tensor_tensor, u, psum[fb][:, 0:NT * H], col("b_f"), ALU.add))
        bank_free[fb] = [m]
        act.wait(m)
        m = act.step(partial(nc.scalar.activation, a, u, ACT.Abs))
        act.wait(m)
        m = act.step(partial(nc.scalar.activation, a, a, ACT.Exp, scale=-1.0))
        dve.wait(m)
        m = dve.step(partial(nc.vector.tensor_scalar, a, a, 1.0, None, ALU.add))
        act.wait(m)
        m = act.step(partial(nc.scalar.activation, l, a, ACT.Ln))
        dve.wait(m)
        m = dve.step(partial(nc.vector.scalar_tensor_tensor, out=logf, in0=u, scalar=0.0, in1=l, op0=ALU.min, op1=ALU.subtract))
        dve.wait(m)
        logf_ready = dve.step(partial(nc.vector.tensor_scalar, nlogf, logf, -1.0, None, ALU.mult))

        qT = work_b[:, 0:AC, :]
        kT = work_b[:, AC:2 * AC, :]
        qk_ready = {}
        heads1 = []

        def scores_first(h):
            q0 = (h % 2) * HD1
            part = slice(q0, q0 + HD1)
            pe.wait(*qk_ready[h // 4], logf_ready)

            def minus_c(i, t):
                for c in range(t + 1):
                    o = psum[i][:, t * P + c * P:t * P + (t + 1) * P]
                    a = nlogf[:, c * H + h:c * H + h + 1].to_broadcast([P, P])
                    b = tri[c][:, c * P:(t + 1) * P]
                    issue = partial(nc.tensor.matmul, o, a, b, start=False, stop=c == t)
                    m = pe.step(issue) if c == t else pe.do(issue)
                return m

            i, m = scores(qT[part, h // 2, :], kT[part, h // 2, :], minus_c)
            add = lambda z, s, t: partial(nc.vector.scalar_tensor_tensor, 
                out=z, in0=s, scalar=c_q[:, t * H + h:t * H + h + 1], in1=mask[:, P:S] if t == 0 else mask,
                op0=ALU.add, op1=ALU.add)
            heads1.append((h, i, m, add))

        attend_bank = {}

        def finish_first():
            h, i, m, add = heads1.pop(0)
            dve.wait(cq_ready)
            b, inv = softmax(i, m, add)
            p_ready = scale_prob(b, inv)
            return h, b, p_ready

        def values_first(h, b, p_ready):
            u, copied = turn_prob(b, p_ready)
            rows = slice((h % 2) * HD1, (h % 2 + 1) * HD1)
            if h % 2 == 0:
                attend_bank[0] = take_bank()
            i = attend_bank[0]
            pe.wait(copied, *values_done)
            o = psum[i]
            v = lambda c: work_v[:, c, h * HD1:(h + 1) * HD1]
            pe.do(partial(nc.tensor.matmul, o[rows, 0:S], v(0), prob_t[u][:, 0:S], start=True, stop=False))
            m = pe.step(partial(nc.tensor.matmul, o[rows, P:S], v(1), prob_t[u][:, S:3 * P], start=False, stop=True))
            prob_t_free[u] = m
            if h % 2 == 1:
                split_bank(i, o[:, 0:S], h // 2, m, y_used[0])
            return m

        y_ready = {}

        def split_bank(i, src, k, done, free, scale=None):
            act.wait(done, free)
            if scale is None:
                hi = act.step(partial(nc.scalar.activation, y_hi[:, k, :], src, ACT.Copy))
                dve.wait(hi, done)
                lo = dve.step(partial(nc.vector.tensor_tensor, y_lo[:, k, :], src, y_hi[:, k, :].bitcast(F32), ALU.subtract))
            else:
                hi = act.step(partial(nc.scalar.activation, y_hi[:, k, :], src, ACT.Copy, scale=scale))
                dve.wait(hi, done)
                lo = dve.step(partial(nc.vector.scalar_tensor_tensor, 
                    out=y_lo[:, k, :], in0=src, scalar=scale, in1=y_hi[:, k, :].bitcast(F32), op0=ALU.mult, op1=ALU.subtract))
            y_ready[k] = (hi, lo)
            bank_free[i] = [hi, lo]

        pair = lambda i: psum[i][:, :].rearrange("p (k n) -> p k n", k=2)
        for g in range(2):
            (i,), m = weights_still("qk1", g, *h_of, ready, KC, 2)
            act.wait(m, *ready(KC - 1))
            q = act.step(partial(nc.scalar.activation, qT[:, 2 * g:2 * g + 2, :], pair(i), ACT.Copy, scale=HD1 ** -0.5))
            bank_free[i] = [q]
            (i,), m = weights_still("qk1", 2 + g, *h_of, ready, KC, 2)
            dve.wait(m)
            k = dve.step(partial(nc.vector.tensor_copy, kT[:, 2 * g:2 * g + 2, :], pair(i)))
            bank_free[i] = [k]
            qk_ready[g] = (q, k)
            if g == 0:
                cb = take_bank()
                pe.wait(logf_ready, const_loaded)
                for t in range(NT):
                    o = psum[cb][:, t * H:(t + 1) * H]
                    for c in range(t + 1):
                        a, b = tri[c][:, t * P:(t + 1) * P], logf[:, c * H:(c + 1) * H]
                        m = pe.step(partial(nc.tensor.matmul, o, a, b, start=c == 0, stop=c == t))
                dve.wait(m)
                cq_ready = dve.step(partial(nc.vector.tensor_copy, c_q[:, :], psum[cb][:, 0:NT * H]))
                bank_free[cb] = [cq_ready]

        zc = bias[:, 0:AC, :]
        ya = bias[:, AC:2 * AC, :]
        waiting = []

        def attend_first(h):
            if h < H:
                scores_first(h)
                waiting.append(finish_first())
            if len(waiting) > 1 or h >= H:
                values_first(*waiting.pop(0))

        conv_free = None
        for g in range(2):
            two = slice(2 * g, 2 * g + 2)
            (i,), m = weights_still("mix", 2 + g, *h_of, ready, KC, 2)
            dve.wait(m)
            a = dve.step(partial(nc.vector.tensor_copy, zc[:, two, :], pair(i)))
            bank_free[i] = [a]
            attend_first(2 * g)
            (i,), m = weights_still("mix", 4 + g, *h_of, ready, KC, 2)
            dve.wait(m, a)
            z_ready = dve.step(partial(nc.vector.tensor_tensor, zc[:, two, :], pair(i), zc[:, two, :], ALU.mult))
            bank_free[i] = [z_ready]
            attend_first(2 * g + 1)
            for j in range(2 * g, 2 * g + 2):
                tap = lambda n, j=j: col("conv", 3 * j + n, 1)
                dve.wait(z_ready)
                m = dve.step(partial(nc.vector.tensor_scalar, ya[:, j, :], zc[:, j, :], tap(2), None, ALU.mult))
                for shift in (1, 2):
                    dve.wait(m)
                    m = dve.step(partial(nc.vector.scalar_tensor_tensor, 
                        out=ya[:, j, shift:S], in0=zc[:, j, 0:S - shift], scalar=tap(2 - shift), in1=ya[:, j, shift:S],
                        op0=ALU.mult, op1=ALU.add))
        conv_done = m
        conv_ready = {}
        for g in range(2):
            two = slice(2 * g, 2 * g + 2)
            to = slice(AC + 2 * g, AC + 2 * g + 2)
            (i,), m = weights_still("mix", g, *h_of, ready, KC, 2)
            dve.wait(m, conv_done)
            full = dve.step(partial(nc.vector.tensor_tensor, ya[:, two, :], pair(i), ya[:, two, :], ALU.mult))
            bank_free[i] = [full]
            act.wait(full, y_used[0])
            hi = act.step(partial(nc.scalar.activation, y_hi[:, to, :], ya[:, two, :], ACT.Copy))
            dve.wait(hi, full)
            lo = dve.step(partial(nc.vector.tensor_tensor, 
                y_lo[:, to, :], ya[:, two, :], y_hi[:, to, :].bitcast(F32), ALU.subtract))
            conv_free = lo
            for k in (2 * g, 2 * g + 1):
                conv_ready[k] = (hi, lo)
            attend_first(4 + 2 * g)
            attend_first(5 + 2 * g)
        attend_first(H)

        gate_c = work_a[:, :].rearrange("p (k n) -> p k n", k=KC)
        gate_a = bias
        gate_ready = {}
        for n, place in enumerate((gate_c, gate_a)):
            for g in range(4):
                (i,), m = weights_still("mix", 6 + 4 * n + g, *h_of, ready, KC, 2)
                act.wait(m, conv_free)
                s = act.step(partial(nc.scalar.activation, 
                    place[:, 2 * g:2 * g + 2, :], pair(i), ACT.Sigmoid))
                bank_free[i] = [s]
                gate_ready[n, g] = s
        h_used[0] = m

        conv_of = (lambda k: y_hi[:, AC + k, :], lambda k: y_lo[:, AC + k, :])
        attn_of = (lambda k: y_hi[:, k, :], lambda k: y_lo[:, k, :])
        merged = {}
        conv_part = {}
        for n in range(2):
            for half in range(2):
                src, rdy = (conv_of, lambda k: conv_ready[k]) if n == 0 else (attn_of, lambda k: y_ready[k])
                banks, m = weights_still("branch", 2 * n + half, *src, rdy, AC, 4)
                for b, i in enumerate(banks):
                    g = 2 * half + b
                    two = slice(2 * g, 2 * g + 2)
                    place = gate_c if n == 0 else gate_a
                    dve.wait(m, gate_ready[n, g])
                    full = dve.step(partial(nc.vector.tensor_tensor, 
                        place[:, two, :], pair(i), place[:, two, :], ALU.mult))
                    bank_free[i] = [full]
                    if n == 0:
                        conv_part[g] = full
                        continue
                    dve.wait(full, conv_part[g])
                    full = dve.step(partial(nc.vector.tensor_tensor, 
                        gate_a[:, two, :], gate_a[:, two, :], gate_c[:, two, :], ALU.add))
                    act.wait(full, h_used[0])
                    hi = act.step(partial(nc.scalar.activation, h_hi[:, two, :], gate_a[:, two, :], ACT.Copy))
                    dve.wait(hi, full)
                    lo = dve.step(partial(nc.vector.tensor_tensor, 
                        h_lo[:, two, :], gate_a[:, two, :], h_hi[:, two, :].bitcast(F32), ALU.subtract))
                    for k in (2 * g, 2 * g + 1):
                        merged[k] = (hi, lo)
        y_used[0] = m
        work_a_used[0] = full
        work_v_used[0] = m

        def wide_product(name, order, tok, rdy):
            done = {}
            for index in order:
                c, half = divmod(index, 2)
                m = weights_moving(name, index, *tok, rdy, KC // 2, 512, lambda t, _: 4 + 2 * t + c, half * KC // 2, KC)
                for t in range(NT):
                    done[t, c] = m[t]
            return [[done[t, c] for c in range(2)] for t in range(NT)]

        marks = wide_product("out1", (0, 2, 1, 3), h_tok, lambda k: merged[k])
        h_used[0] = marks[1][1]
        x_ready = post_norm(marks, 0)
        load_gain(0, dram["norm_g"][0, 3])
        ready = pre_norm(x_ready, col("ffn_pre"), None, [])
        marks = feed_forward("gate_up1", "down1", 0, ready)
        x_ready = post_norm(marks, 1)
        load_gain(1, dram["norm_g"][1, 1])

        table, hot = prob[0][0:BUCKETS + 1, 0:H], prob[1][0:BUCKETS + 1, :]
        pool.wait(prob_free[0], prob_free[1])
        pool.dma(partial(nc.gpsimd.dma_start, table, dram["rel_table"]), table_in)
        loaded = pool.dma(partial(nc.gpsimd.dma_start, hot, dram["bucket_of"]), table_in)
        i = take_bank()
        pe.wait(loaded)
        m = pe.step(partial(nc.tensor.matmul, psum[i][0:H, 0:BIAS_W], table, hot, start=True, stop=True))
        dve.wait(m, prob_free[2])
        rows = dve.step(partial(nc.vector.tensor_copy, prob[2][0:H, :], psum[i][0:H, 0:BIAS_W]))
        bank_free[i] = [rows]
        pool.wait(rows)
        kept = pool.dma(partial(nc.gpsimd.dma_start, bias_dram, prob[2][0:H, :]), bias_sig)
        pool.wait(kept, work_a_used[0])
        diagonal = bass.AP(bias_dram.tensor, 0, [[1, P], [BIAS_W, H], [1, S]])
        diagonal_in = pool.dma(partial(nc.gpsimd.dma_start, bias[:, :, :], diagonal), bias_sig)
        bias_ready = []
        pe.wait(diagonal_in)
        for h in range(0, H, 2):
            i = take_bank()
            two = bias[:, h:h + 2, :]
            flipped = pe.step(partial(nc.tensor.matmul, pair(i), flip, two, start=True, stop=True))
            dve.wait(flipped)
            bias_ready.append(dve.step(partial(nc.vector.tensor_copy, two, pair(i))))
            bank_free[i] = [bias_ready[-1]]
        prob_free[0] = prob_free[1] = m
        prob_free[2] = kept

        l0 = COLUMNS["lam"][0]
        quarter = lambda n: cols[:, l0 + n * DIFF:l0 + (n + 1) * DIFF]
        for n in range(2):
            m = dve.step(partial(nc.vector.tensor_tensor, 
                lam_pr[:, n * DIFF:(n + 1) * DIFF], quarter(2 * n), quarter(2 * n + 1), ALU.mult))
        dve.wait(m)
        m = dve.step(partial(nc.vector.tensor_reduce, 
            lam_sb[:, 0:2], lam_pr[:, :].rearrange("p (a n) -> p a n", a=2), AX_X, ALU.add))
        act.wait(m)
        m = act.step(partial(nc.scalar.activation, lam_sb[:, 0:2], lam_sb[:, 0:2], ACT.Exp))
        dve.wait(m)
        m = dve.step(partial(nc.vector.scalar_tensor_tensor, 
            out=lam_sb[:, 2:3], in0=lam_sb[:, 0:1], scalar=LAMBDA_INIT, in1=lam_sb[:, 1:2], op0=ALU.add, op1=ALU.subtract))
        lam_ready = m
        dve.do(partial(nc.vector.tensor_scalar, subln_sc[:, :], col("subln"), 1.0 - LAMBDA_INIT, None, ALU.mult))

        for layer, name in enumerate(("moba", "diff")):
            q_scale = (HD2 if layer == 0 else DIFF) ** -0.5
            scale, shift = mod_cols[:, 4 * layer, :], mod_cols[:, 4 * layer + 1, :]
            ready = pre_norm(x_ready, scale, shift, [mod_ready[layer, 0, 0], mod_ready[layer, 0, 1]])
            values_done = token_values(name + "_v", 2, ready, D)
            q_all, k_all = work_b, work_a[:, :].rearrange("p (k n) -> p k n", k=KC)
            qk_ready = {}
            scored, softened = [], []
            y_ready.clear()

            def score_head(h):
                pe.wait(*qk_ready[h // 2])
                halves = 1 if layer == 0 else 2
                width = P // halves
                got = []
                for c in range(halves):
                    part = slice(c * width, (c + 1) * width)
                    i, m = scores(q_all[part, h, :], k_all[part, h, :])
                    b0 = bias[:, h, P:S]
                    b1 = bias[:, h, :]
                    dve.wait(bias_ready[-1])
                    add = lambda z, s, t, b0=b0, b1=b1: partial(nc.vector.tensor_tensor, z, s, b0 if t == 0 else b1, ALU.add)
                    got.append(softmax(i, m, add))
                b, inv = got[0]
                last = scale_prob(b, inv)
                if layer == 1:
                    b2, inv2 = got[1]
                    s2 = soft[:, b2, :]
                    dve.wait(inv2, lam_ready)
                    m2 = dve.step(partial(nc.vector.tensor_scalar, s2[:, 4:6], s2[:, 4:6], lam_sb[:, 2:3], -1.0, ALU.mult, ALU.mult))
                    dve.wait(m2, last)
                    for t, w in enumerate((W0, W1)):
                        last = dve.step(partial(nc.vector.scalar_tensor_tensor, 
                            out=prob[b][:, w], in0=prob[b2][:, w], scalar=s2[:, 4 + t:5 + t], in1=prob[b][:, w],
                            op0=ALU.mult, op1=ALU.add))
                    prob_free[b2] = last
                softened.append((h, b, last, m))

            def apply_head():
                h, b, p_ready, scored_mark = softened.pop(0)
                u, copied = turn_prob(b, p_ready)
                i = take_bank()
                pe.wait(copied, *values_done)
                v = lambda c: work_v[:, c, h * P:(h + 1) * P]
                o = psum[i]
                if layer == 0:
                    pe.do(partial(nc.tensor.matmul, o[:, 0:S], v(0), prob_t[u][:, 0:S], start=True, stop=False))
                    m = pe.step(partial(nc.tensor.matmul, o[:, P:S], v(1), prob_t[u][:, S:3 * P], start=False, stop=True))
                    prob_t_free[u] = m
                    split_bank(i, o[:, 0:S], h, m, y_used[0])
                    return m
                pe.do(partial(nc.tensor.matmul, o[:, 0:P], prob_t[u][:, 0:P], v(0), start=True, stop=True))
                pe.do(partial(nc.tensor.matmul, o[:, P:S], prob_t[u][:, P:S], v(0), start=True, stop=False))
                m = pe.step(partial(nc.tensor.matmul, o[:, P:S], prob_t[u][:, S:3 * P], v(1), start=False, stop=True))
                prob_t_free[u] = m
                dve.wait(m, scored_mark)
                o_copied = dve.step(partial(nc.vector.tensor_copy, work_b[:, h, :], o[:, 0:S]))
                bank_free[i] = [o_copied]
                act.wait(o_copied, prob_junk_free[0])
                for t in range(NT):
                    sq = act.step(partial(nc.scalar.activation, 
                        lam_pr[:, :], work_b[:, h, t * P:(t + 1) * P], ACT.Square, accum_out=diff_stat[:, 0, NT * h + t:NT * h + t + 1]))
                    act.wait(sq)
                diff_squares[h] = sq
                return m

            diff_squares = {}
            prob_junk_free = [lam_ready]

            def norm_heads(heads):
                n0, n1 = NT * heads[0], NT * heads[-1] + NT
                r = inverse_rms(diff_stat[:, 0, n0:n1], HD2, n1 - n0, [diff_squares[h] for h in heads])
                dve.wait(r)
                for h in heads:
                    for t in range(NT):
                        s = dve.step(partial(nc.vector.tensor_scalar, 
                            work_b[:, h, t * P:(t + 1) * P], work_b[:, h, t * P:(t + 1) * P],
                            diff_stat[:, 0, NT * h + t:NT * h + t + 1], None, ALU.mult))
                    i = take_bank()
                    pe.wait(s)
                    for t in range(NT):
                        m = pe.step(partial(nc.tensor.transpose, 
                            psum[i][:, t * P:(t + 1) * P], work_b[:, h, t * P:(t + 1) * P], ident))
                    split_bank(i, psum[i][:, 0:S], h, m, y_used[0], scale=subln_sc[:, 0:1])

            for g in range(4):
                two = slice(2 * g, 2 * g + 2)
                (i,), m = weights_still(name + "_qk", g, *h_of, ready, KC, 2)
                act.wait(m, *ready(KC - 1))
                q = act.step(partial(nc.scalar.activation, q_all[:, two, :], pair(i), ACT.Copy, scale=q_scale))
                bank_free[i] = [q]
                if g:
                    score_head(2 * g - 2)
                (i,), m = weights_still(name + "_qk", 4 + g, *h_of, ready, KC, 2)
                act.wait(m, work_a_used[0])
                k = act.step(partial(nc.scalar.activation, k_all[:, two, :], pair(i), ACT.Copy))
                bank_free[i] = [k]
                qk_ready[g] = (q, k)
                h_used[0] = m
                if g:
                    apply_head()
                    score_head(2 * g - 1)
                    apply_head()
            score_head(H - 2)
            score_head(H - 1)
            if layer == 1:
                norm_heads(range(0, H - 2))
            apply_head()
            m = apply_head()
            if layer == 1:
                norm_heads(range(H - 2, H))
            work_a_used[0] = m
            work_v_used[0] = m
            marks = wide_product(name + "_o", (0, 2, 1, 3), y_tok, lambda k: y_ready[k])
            y_used[0] = marks[1][1]
            slot = gain_slot[layer, 0]
            x_ready = post_norm(marks, slot)
            if layer == 0:
                load_gain(slot, dram["norm_g"][1, 3])
            scale, shift = mod_cols[:, 4 * layer + 2, :], mod_cols[:, 4 * layer + 3, :]
            ready = pre_norm(x_ready, scale, shift, [mod_ready[layer, 1, 0], mod_ready[layer, 1, 1]])
            marks = feed_forward("gate_up2", "down2", layer, ready)
            x_ready = post_norm(marks, gain_slot[layer, 1])

        for t in range(NT):
            sync.wait(x_ready[t])
            done = sync.dma(partial(nc.sync.dma_start, out[t * P:(t + 1) * P, :], x_res[:, t, :]), stored)
        sync.wait(done)

        block = ctx.enter_context(nc.Block())

        @block.sync
        def _(e):
            sync.play(e)

        @block.scalar
        def _(e):
            act.play(e)

        @block.vector
        def _(e):
            dve.play(e)

        @block.gpsimd
        def _(e):
            pool.play(e)

        @block.tensor
        def _(e):
            pe.play(e)


def kernel(**inputs):
    import numpy as np
    import concourse.bacc as bacc
    from concourse.bass_utils import run_bass_kernel_spmd as run

    a = {name: np.asarray(value) for name, value in inputs.items()}
    put = np.ascontiguousarray

    def slabs(w, kcs, width):
        K, N = w.shape
        return put(w.reshape(K // (P * kcs), kcs, P, N // width, width).transpose(3, 0, 2, 1, 4)).reshape(-1, P, kcs * width)

    def columns(v):
        return v.reshape(-1, P).T

    w_in = a["w_in"][0]
    rest = 3 * AW + H
    qkv = {"moba": a["moba_w_qkv_2"][0], "diff": a["diff_w_qkv_2"][0]}
    rel = (BIAS_W - P - 1) - np.arange(BIAS_W)
    n = np.maximum(rel, 1).astype(np.float32)
    half = BUCKETS // 2
    far = half + (np.log(n / half) / math.log(2048 / half) * (BUCKETS - half)).astype(np.int32)
    bucket = np.where(rel < half, rel, np.minimum(far, BUCKETS - 1))
    bucket = np.where(rel < 0, BUCKETS, bucket)
    bucket_of = (bucket[None, :] == np.arange(BUCKETS + 1)[:, None]).astype(np.float32)
    const = np.zeros((P, N_CONST), np.float32)
    row, s = np.arange(P)[:, None], np.arange(S)[None, :]
    const[:, IDENT:IDENT + P] = np.eye(P)
    const[:, ONES:ONES + P] = 1.0
    const[:, FLIP:FLIP + P] = np.eye(P)[::-1]
    for c in range(NT):
        const[:, TRI + c * S:TRI + (c + 1) * S] = c * P + row <= s
    const[:, MASK:MASK + S] = np.where(s > row + P, NEG, 0.0)
    small = {
        "mix_pre": columns(a["norm_mix_pre"][0]), "ffn_pre": columns(a["norm_ffn_pre"][0]), "c": columns(a["c_2"][0]),
        "g00": columns(a["norm_g_2"][0, 0]), "g02": columns(a["norm_g_2"][0, 2]),
        "g10": columns(a["norm_g_2"][1, 0]), "g12": columns(a["norm_g_2"][1, 2]),
        "conv": a["conv_w"][0].reshape(3, AC, P).transpose(2, 1, 0).reshape(P, 3 * AC),
        "subln": columns(a["diff_subln_g_2"][0]),
        "b_f": np.broadcast_to(np.concatenate([a["b_f"][0]] * NT)[None, :], (P, NT * H)),
        "lam": np.broadcast_to(a["diff_lambda_2"][0].reshape(1, -1), (P, 4 * DIFF)),
    }
    arrays = {
        "x": a["x"][0],
        "cols": np.concatenate([small[k] for k in COLUMNS], axis=1),
        "const": const,
        "bucket_of": bucket_of,
        "rel_table": np.concatenate([a["rel_bias_2"], np.full((1, H), NEG, np.float32)], axis=0),
        "wf": w_in[:, 3 * AW:rest].reshape(KC, P, H).transpose(1, 0, 2).reshape(P, KC * H),
        "qk1": slabs(w_in[:, 0:2 * AW], KC, 256),
        "v1": slabs(w_in[:, 2 * AW:3 * AW], KC // 2, 512),
        "mix": slabs(w_in[:, rest:], KC, 256),
        "branch": np.concatenate([slabs(a["w_branch"][0, i], AC, 512) for i in range(2)]),
        "out1": slabs(a["w_out"][0], KC // 2, 512),
        "gate_up1": slabs(a["w_gate_up"][0], KC, 256),
        "down1": slabs(a["w_down"][0], 2, D),
        "gate_up2": np.concatenate([slabs(a["ffn_w_in_2"][i], KC, 256) for i in range(2)]),
        "down2": np.concatenate([slabs(a["ffn_w_out_2"][i], 2, D) for i in range(2)]),
        "ada": np.concatenate([slabs(a["ada_w_2"][i], 1, SLAB) for i in range(2)]),
        "ada_b": a["ada_b_2"].reshape(-1, SLAB),
        "mix_post": a["norm_mix_post"], "ffn_post": a["norm_ffn_post"], "norm_g": a["norm_g_2"],
    }
    for name, w in qkv.items():
        arrays[name + "_qk"] = slabs(w[:, 0:2 * D], KC, 256)
        arrays[name + "_v"] = slabs(w[:, 2 * D:], KC // 2, 512)
        arrays[name + "_o"] = slabs(a[name + "_w_o_2"][0], KC // 2, 512)

    nc = bacc.Bacc("TRN2", target_bir_lowering=False, num_devices=1, dynamic_dma_scratch_size=2048)
    arrays = {"in_" + k: put(v) for k, v in arrays.items()}
    dram = {k[3:]: nc.dram_tensor(k, v.shape, mybir.dt.from_np(v.dtype), kind="ExternalInput").ap() for k, v in arrays.items()}
    out = nc.dram_tensor("out", (S, D), F32, kind="ExternalOutput").ap()
    build_program(nc, dram, out)
    result = run(nc, [arrays], core_ids=[0])
    return result.results[0]["out"].reshape(1, S, D)
```

```python
import math
from contextlib import ExitStack
from functools import partial

import concourse.bass as bass
from concourse import mybir

F32 = mybir.dt.float32
F32R = mybir.dt.float32r
ALU = mybir.AluOpType
ACT = mybir.ActivationFunctionType
AX_X = mybir.AxisListType.X

P = 128
S = 256
NT = S // P
D = 1024
KC = D // P
H = 8
HD1 = 64
AW = H * HD1
AC = AW // P
HD2 = D // H
DIFF = HD2 // 2
FF = -(-8 * D // (3 * 256)) * 256
FG = FF // 256
BUCKETS = 32
EPS = 1e-6
NEG = -1e30
LAMBDA_INIT = 0.8 - 0.6 * math.exp(-0.3 * 1)

SLAB = 2048
N_RAW, N_HI, N_LO = 6, 4, 4
AHEAD = 3

COLUMNS = {}
for _name, _n in (("mix_pre", KC), ("ffn_pre", KC), ("c", KC), ("g00", KC), ("g02", KC), ("g10", KC), ("g12", KC),
                  ("conv", 3 * AC), ("subln", 1), ("b_f", NT * H), ("lam", 4 * DIFF)):
    COLUMNS[_name] = (sum(w for _, w in COLUMNS.values()), _n)
N_COLUMNS = sum(w for _, w in COLUMNS.values())

IDENT, ONES, FLIP, TRI = 0, P, 2 * P, 3 * P
MASK = TRI + NT * S
N_CONST = MASK + S
BIAS_W = 3 * P


class Mark:

    def __init__(self, sem, value):
        self.sem, self.value = sem, value


class Counter:

    def __init__(self, sem):
        self.sem, self.count = sem, 0

    def step(self, n):
        self.count += n
        return Mark(self.sem, self.count)


class Queue:

    def __init__(self, counter):
        self.counter, self.items, self.seen = counter, [], {}

    def wait(self, *marks):
        for m in marks:
            if m is not None and self.seen.get(id(m.sem), 0) < m.value:
                self.seen[id(m.sem)] = m.value
                self.items.append((None, m.sem, m.value))

    def do(self, issue):
        self.items.append((issue, None, 0))

    def step(self, issue):
        m = self.counter.step(1)
        self.items.append((issue, m.sem, 1))
        return m

    def dma(self, issue, counter):
        m = counter.step(16)
        self.items.append((issue, m.sem, 16))
        return m

    def play(self, engine):
        for issue, sem, n in self.items:
            if issue is None:
                engine.wait_ge(sem, n)
            elif sem is None:
                issue()
            else:
                issue().then_inc(sem, n)


def slab_order():
    def ffn(gate_up, down, base):
        order = []
        for g in range(FG):
            order += [(gate_up, base * 2 * FG + g), (gate_up, base * 2 * FG + FG + g)]
            if g:
                order.append((down, base * FG + g - 1))
        return order + [(down, base * FG + FG - 1)]

    order = [("v1", 0), ("v1", 1)]
    for i in range(2):
        order += [("qk1", i), ("qk1", 2 + i)]
    order += [("mix", 2), ("mix", 4), ("mix", 3), ("mix", 5), ("mix", 0), ("mix", 1)]
    order += [("mix", 6 + i) for i in range(8)]
    order += [("branch", i) for i in range(4)] + [("out1", i) for i in (0, 2, 1, 3)]
    order += ffn("gate_up1", "down1", 0)
    for i, name in enumerate(("moba", "diff")):
        for j in range(4):
            order += [(name + "_qk", j), (name + "_qk", 4 + j)]
        order += [(name + "_v", j) for j in range(4)]
        order += [(name + "_o", j) for j in (0, 2, 1, 3)]
        order += ffn("gate_up2", "down2", i)
    return order


def build_program(nc, dram, out):
    with ExitStack() as ctx:
        def sb(name, shape, dt=F32):
            return ctx.enter_context(nc.sbuf_tensor(name, shape, dt))

        def sem(name):
            return ctx.enter_context(nc.semaphore(name))

        raw = [sb(f"raw{i}", [P, SLAB]) for i in range(N_RAW)]
        high = [sb(f"high{i}", [P, SLAB], F32R) for i in range(N_HI)]
        low = [sb(f"low{i}", [P, SLAB], F32R) for i in range(N_LO)]
        x_res = sb("x_res", [P, NT, D])
        h_hi = sb("h_hi", [P, KC, S], F32R)
        h_lo = sb("h_lo", [P, KC, S], F32R)
        y_hi = sb("y_hi", [P, KC, S], F32R)
        y_lo = sb("y_lo", [P, KC, S], F32R)
        work = sb("work", [P, 2 * NT * D])
        work_a = work[:, 0:NT * D]
        work_b = work[:, NT * D:].rearrange("p (k n) -> p k n", k=KC)
        work_v = sb("work_v", [P, NT, D])
        bias = sb("bias", [P, H, S])
        work_b_flat = work[:, NT * D:]
        gain = [sb(f"gain{i}", [P, D]) for i in range(3)]
        ada = sb("ada", [P, SLAB])
        prob = [sb(f"prob{i}", [P, 3 * P]) for i in range(4)]
        prob_t = [sb(f"prob_t{i}", [P, 3 * P]) for i in range(2)]
        const = sb("const", [P, N_CONST])
        cols = sb("cols", [P, N_COLUMNS])
        c_act = sb("c_act", [P, KC])
        mod_cols = sb("mod_cols", [P, 8, KC])
        stat = sb("stat", [P, 32])
        soft = sb("soft", [P, 4, 8])
        lam_sb = sb("lam_sb", [P, 4])
        lam_pr = sb("lam_pr", [P, 2 * DIFF])
        subln_sc = sb("subln_sc", [P, 1])
        wf_raw = sb("wf_raw", [P, KC * H])
        wf_hi = sb("wf_hi", [P, KC * H], F32R)
        wf_lo = sb("wf_lo", [P, KC * H], F32R)
        gate_f = sb("gate_f", [P, 5, NT * H])
        c_q = sb("c_q", [P, NT * H])
        diff_stat = sb("diff_stat", [P, NT * H])
        psum = [ctx.enter_context(nc.psum_tensor(f"psum{i}", [P, 512], F32)) for i in range(8)]
        bias_dram = nc.dram_tensor("bias_dram", (H, BIAS_W), F32, kind="Internal").ap()

        pe = Queue(Counter(sem("pe_done")))
        act = Queue(Counter(sem("act_done")))
        dve = Queue(Counter(sem("dve_done")))
        pool = Queue(Counter(sem("pool_done")))
        sync = Queue(None)
        raw_in = [Counter(sem(f"raw_in{i}")) for i in range(N_RAW)]
        x_in = [Counter(sem(f"x_in{t}")) for t in range(NT)]
        const_in, cols_in, wf_in = (Counter(sem(n)) for n in ("const_in", "cols_in", "wf_in"))
        bias_sig = Counter(sem("bias_sig"))
        table_in = Counter(sem("table_in"))
        ada_in = Counter(sem("ada_in"))
        gain_in = [Counter(sem(f"gain_in{i}")) for i in range(3)]
        stored = Counter(sem("stored"))

        ident = const[:, IDENT:IDENT + P]
        ones = const[:, ONES:ONES + P]
        flip = const[:, FLIP:FLIP + P]
        tri = [const[:, TRI + c * S:TRI + (c + 1) * S] for c in range(NT)]
        mask = const[:, MASK:MASK + S]

        def col(name, a=0, n=None):
            o, w = COLUMNS[name]
            return cols[:, o + a:o + a + (w if n is None else n)]

        x_loaded = [sync.dma(partial(nc.sync.dma_start, x_res[:, t, :], dram["x"][t * P:(t + 1) * P, :]), x_in[t]) for t in range(NT)]
        cols_loaded = act.dma(partial(nc.scalar.dma_start, cols[:, :], dram["cols"]), cols_in)

        bank_free = [[] for _ in range(8)]
        turn = [0]

        def take_bank():
            i = turn[0] % 4
            turn[0] += 1
            pe.wait(*bank_free[i])
            bank_free[i] = []
            return i

        main = slab_order()
        first_of = {key: main.index(key) for key in (("gate_up1", 0), ("moba_qk", 0), ("gate_up2", 0), ("diff_qk", 0))}
        turn1, turn2, turn3, turn4 = sorted(first_of.values())
        ada_plan = [(1, turn1 - 2, True), (turn1 + 4, turn1 + 15, False), (turn1 + 19, turn2 - 2, True),
                    (turn2 + 4, turn3 - 2, True), (turn3 + 4, turn3 + 15, False), (turn3 + 19, turn4 - 2, True)]
        after_main = {}
        for b, (lo, hi, _) in enumerate(ada_plan):
            for k in range(KC):
                at = lo + k * (hi - lo) // (KC - 1) if b else (4 + k if k < 2 else 14 + 2 * (k - 2))
                after_main.setdefault(at, []).append(b * KC + k)
        stream = []
        for m in range(len(main)):
            stream += [("main", m)] + [("ada", n) for n in after_main.get(m, [])]
        raw_free = [None] * N_RAW
        loads = [0]
        raw_loaded = {}

        def load_next():
            i = loads[0]
            if i >= len(stream):
                return
            loads[0] += 1
            kind, n = stream[i]
            src = dram["ada"][n] if kind == "ada" else dram[main[n][0]][main[n][1]]
            slot = i % N_RAW
            sync.wait(raw_free[slot])
            raw_loaded[i] = sync.dma(partial(nc.sync.dma_start, raw[slot][:, :], src), raw_in[slot])

        slab_used = {}
        slab_split = {}
        done_items = [0]
        pending, at_norm = [], []
        ada_state = {"init": None, "free": None}

        def split_next():
            i = done_items[0]
            done_items[0] += 1
            kind, n = stream[i]
            slot = i % N_RAW
            src = raw[slot]
            if kind == "main":
                hi, lo = high[n % N_HI], low[n % N_LO]
                act.wait(raw_loaded[i], slab_used.get(n - N_HI))
                rounded = act.step(partial(nc.scalar.activation, hi[:, :], src[:, :], ACT.Copy))
                dve.wait(rounded, slab_used.get(n - N_LO))
                rest = dve.step(partial(nc.vector.tensor_tensor, lo[:, :], src[:, :], hi[:, :].bitcast(F32), ALU.subtract))
                slab_split[n] = (rounded, rest)
                raw_free[slot] = rest
            else:
                block, k = divmod(n, KC)
                if k == 0:
                    assert not pending and not at_norm
                    pool.wait(ada_state["free"])
                    cleared = pool.step(partial(nc.gpsimd.memset, ada[:, :], 0.0))
                    pool.wait(cleared)
                    ada_state["init"] = pool.dma(partial(nc.gpsimd.dma_start, ada[0:1, :], dram["ada_b"][block:block + 1, :]), ada_in)
                dve.wait(raw_loaded[i], ada_state["init"], c_ready)
                summed = dve.step(partial(nc.vector.scalar_tensor_tensor, 
                    out=ada[:, :], in0=src[:, :], scalar=c_act[:, k:k + 1], in1=ada[:, :], op0=ALU.mult, op1=ALU.add))
                ada_state["init"] = summed
                raw_free[slot] = summed
                if k == KC - 1:
                    (at_norm if ada_plan[block][2] else pending).append(partial(finish_ada, block, summed))
            load_next()

        used = [0]

        def next_slab(name, index, ahead=AHEAD):
            n = used[0]
            used[0] += 1
            assert main[n] == (name, index), (main[n], name, index)
            while (n + ahead not in slab_split) and done_items[0] < len(stream):
                split_next()
            pe.wait(*slab_split[n])
            return n, high[n % N_HI], low[n % N_LO]

        def slab_done(n, mark):
            slab_used[n] = mark
            while pending:
                pending.pop(0)()

        def weights_still(name, index, hi, lo, ready, kcs, n_chunks):
            n, wh, wl = next_slab(name, index)
            wh = wh[:, :].rearrange("p (k n) -> p k n", k=kcs)
            wl = wl[:, :].rearrange("p (k n) -> p k n", k=kcs)
            banks = []
            for j in range(n_chunks):
                if j % 2 == 0:
                    banks.append(take_bank())
                o = psum[banks[-1]][:, (j % 2) * S:(j % 2 + 1) * S]
                for k in range(kcs):
                    pe.wait(*ready(k))
                    a, b = wh[:, k, j * P:(j + 1) * P], wl[:, k, j * P:(j + 1) * P]
                    first, last = k == 0, k == kcs - 1
                    pe.do(partial(nc.tensor.matmul, o, a, hi(k), start=first, stop=False))
                    pe.do(partial(nc.tensor.matmul, o, a, lo(k), start=False, stop=False))
                    issue = partial(nc.tensor.matmul, o, b, hi(k), start=False, stop=last)
                    if last and (j % 2 == 1 or j == n_chunks - 1):
                        mark = pe.step(issue)
                    else:
                        pe.do(issue)
            slab_done(n, mark)
            return banks, mark

        def weights_moving(name, parts, hi, lo, ready, kcs, k_all):
            slabs = []
            for i, (index, k0, blocks) in enumerate(parts):
                n, wh, wl = next_slab(name, index, AHEAD - i)
                slabs.append((n, k0, blocks, *(w[:, :].rearrange("p (k n) -> p k n", k=kcs) for w in (wh, wl))))
            marks = {}
            for t in range(NT):
                for n, k0, blocks, wh, wl in slabs:
                    for j, c in enumerate(blocks):
                        o = psum[4 + 2 * t + c][:, :]
                        for k in range(kcs):
                            pe.wait(*ready(k0 + k))
                            a, b = hi(k0 + k, t), lo(k0 + k, t)
                            vh, vl = wh[:, k, j * 512:(j + 1) * 512], wl[:, k, j * 512:(j + 1) * 512]
                            first, last = k0 + k == 0, k0 + k == k_all - 1
                            if first:
                                pe.wait(*bank_free[4 + 2 * t + c])
                                bank_free[4 + 2 * t + c] = []
                            pe.do(partial(nc.tensor.matmul, o, a, vh, start=first, stop=False))
                            pe.do(partial(nc.tensor.matmul, o, a, vl, start=False, stop=False))
                            issue = partial(nc.tensor.matmul, o, b, vh, start=False, stop=last)
                            if k == kcs - 1:
                                marks[t, c] = pe.step(issue)
                            else:
                                pe.do(issue)
                    if t == NT - 1:
                        slab_done(n, marks[t, blocks[-1]])
            return marks

        gain_ready = [None] * 3
        gain_used = [None] * 3

        def load_gain(slot, src):
            pool.wait(gain_used[slot])
            gain_used[slot] = None
            gain_ready[slot] = pool.dma(partial(nc.gpsimd.dma_start, gain[slot][:, :], src.partition_broadcast(P)), gain_in[slot])

        gain_slot = {(0, 0): 2, (0, 1): 0, (1, 0): 1, (1, 1): 2}
        mod_ready = {}

        def finish_ada(block, summed):
            layer, b = divmod(block, 3)
            last = None
            pe.wait(summed)
            for half in range(2):
                section = 2 * b + half
                part, what = divmod(section, 3)
                if what < 2:
                    i = take_bank()
                    for k in range(KC):
                        a = ada[:, half * D + k * P:half * D + (k + 1) * P]
                        issue = partial(nc.tensor.matmul, psum[i][:, k:k + 1], a, ones[:, 0:1], start=True, stop=True)
                        last = pe.step(issue) if k == KC - 1 else pe.do(issue)
                    dve.wait(last)
                    place = mod_cols[:, 4 * layer + 2 * part + (1 - what), :]
                    if what == 0:
                        got = dve.step(partial(nc.vector.tensor_copy, place, psum[i][:, 0:KC]))
                    else:
                        g = col(f"g{layer}{2 * part}")
                        got = dve.step(partial(nc.vector.scalar_tensor_tensor, 
                            out=place, in0=psum[i][:, 0:KC], scalar=1.0, in1=g, op0=ALU.add, op1=ALU.mult))
                    bank_free[i] = [got]
                    mod_ready[layer, part, what] = got
                else:
                    slot = gain_slot[layer, part]
                    assert gain_used[slot] is None and gain_ready[slot] is not None
                    for c in range(2):
                        i = take_bank()
                        a = ada[:, half * D + c * 512:half * D + (c + 1) * 512]
                        last = pe.step(partial(nc.tensor.matmul, psum[i][:, :], ones, a, start=True, stop=True))
                        dve.wait(last, gain_ready[slot])
                        g = gain[slot][:, c * 512:(c + 1) * 512]
                        got = dve.step(partial(nc.vector.tensor_tensor, g, psum[i][:, :], g, ALU.mult))
                        bank_free[i] = [got]
                    gain_ready[slot] = got
            ada_state["free"] = last

        minus_half = sb("minus_half", [P, NT * H])
        halves_ready = pool.step(partial(nc.gpsimd.memset, minus_half[:, :], -0.5))

        def inverse_rms(sums, n, given):
            pool.wait(given, halves_ready)
            return pool.step(partial(nc.gpsimd.tensor_tensor, sums, sums, minus_half[:, 0:n], ALU.pow))

        h_used = [None]
        work_used = [None]

        def square_halves(src, ready, junk, t, base):
            got = []
            for c in range(2):
                act.wait(ready[c])
                got.append(act.step(partial(
                    nc.scalar.activation, junk[:, (2 * t + c) * 512:(2 * t + c + 1) * 512], src(c), ACT.Square, scale=D ** -0.5,
                    accum_out=stat[:, base + 2 * t + c:base + 2 * t + c + 1])))
            return got

        def join_halves(squares, t, base):
            a = stat[:, base + 2 * t:base + 2 * t + 1]
            dve.wait(*squares)
            m = dve.step(partial(nc.vector.scalar_tensor_tensor, out=a, in0=a, scalar=EPS,
                                 in1=stat[:, base + 2 * t + 1:base + 2 * t + 2], op0=ALU.add, op1=ALU.add))
            return a, inverse_rms(a, 1, m)

        def pre_norm(x_ready, scale, shift, given, meanwhile=None):
            r = []
            for t in range(NT):
                squares = square_halves(lambda c: x_res[:, t, c * 512:(c + 1) * 512], x_ready[t], work_b_flat, t, 0)
                r.append(join_halves(squares, t, 0))
            normed = []
            for t in range(NT):
                dve.wait(r[t][1])
                normed.append(dve.step(partial(
                    nc.vector.tensor_scalar, work_a[:, t * D:(t + 1) * D], x_res[:, t, :], r[t][0], None, ALU.mult)))
            if meanwhile:
                meanwhile()
            banks, turned = [], []
            pe.wait(const_loaded)
            for b in range(KC // 2):
                banks.append(take_bank())
                for t in range(NT):
                    pe.wait(normed[t])
                    for k in (2 * b, 2 * b + 1):
                        o = psum[banks[b]][:, (k % 2) * S + t * P:(k % 2) * S + (t + 1) * P]
                        issue = partial(nc.tensor.transpose, o, work_a[:, t * D + k * P:t * D + (k + 1) * P], ident)
                        m = pe.step(issue) if t == NT - 1 and k % 2 else pe.do(issue)
                turned.append(m)
            ready = []
            for b in range(KC // 2):
                two = slice(2 * b, 2 * b + 2)
                act.wait(turned[b], *given)
                for k in (2 * b, 2 * b + 1):
                    o = psum[banks[b]][:, (k % 2) * S:(k % 2 + 1) * S]
                    if shift is None:
                        full = act.step(partial(nc.scalar.activation, work_b[:, k, :], o, ACT.Copy, scale=scale[:, k:k + 1]))
                    else:
                        full = act.step(partial(nc.scalar.activation, work_b[:, k, :], o, ACT.Identity,
                                                scale=scale[:, k:k + 1], bias=shift[:, k:k + 1]))
                bank_free[banks[b]] = [full]
                dve.wait(full, h_used[0])
                hi = dve.step(partial(nc.vector.tensor_copy, h_hi[:, two, :], work_b[:, two, :]))
                dve.wait(hi)
                lo = dve.step(partial(
                    nc.vector.tensor_tensor, h_lo[:, two, :], work_b[:, two, :], h_hi[:, two, :].bitcast(F32), ALU.subtract))
                ready += [(hi, lo)] * 2
            work_used[0] = lo
            return lambda k: ready[k]

        def post_norm(marks, slot):
            act.wait(work_used[0])
            dve.wait(work_used[0], gain_ready[slot])
            result = []
            for t in range(NT):
                squares = []
                for c in range(2):
                    act.wait(marks[t, c])
                    squares.append(act.step(partial(
                        nc.scalar.activation, work_b_flat[:, (2 * t + c) * 512:(2 * t + c + 1) * 512],
                        psum[4 + 2 * t + c][:, :], ACT.Square, scale=D ** -0.5,
                        accum_out=stat[:, 4 + 2 * t + c:5 + 2 * t + c])))
                a, r = join_halves(squares, t, 4)
                for c in range(2):
                    dve.wait(squares[c])
                    gained = dve.step(partial(
                        nc.vector.tensor_tensor, work_a[:, (2 * t + c) * 512:(2 * t + c + 1) * 512],
                        psum[4 + 2 * t + c][:, :], gain[slot][:, c * 512:(c + 1) * 512], ALU.mult))
                    bank_free[4 + 2 * t + c] = [squares[c], gained]
                dve.wait(r, gained)
                result.append([dve.step(partial(
                    nc.vector.scalar_tensor_tensor, out=x_res[:, t, c * 512:(c + 1) * 512],
                    in0=work_a[:, (2 * t + c) * 512:(2 * t + c + 1) * 512], scalar=a,
                    in1=x_res[:, t, c * 512:(c + 1) * 512], op0=ALU.mult, op1=ALU.add)) for c in range(2)])
            gain_used[slot] = gained
            gain_ready[slot] = None
            while at_norm:
                at_norm.pop(0)()
            return result

        h_of = (lambda k: h_hi[:, k, :], lambda k: h_lo[:, k, :])
        h_tok = (lambda k, t: h_hi[:, k, t * P:(t + 1) * P], lambda k, t: h_lo[:, k, t * P:(t + 1) * P])
        y_tok = (lambda k, t: y_hi[:, k, t * P:(t + 1) * P], lambda k, t: y_lo[:, k, t * P:(t + 1) * P])

        y_used = [None]
        work_v_used = [None]

        def feed_forward(gate_up, down, base, ready, meanwhile={}):
            hidden_ready, hidden_used = {}, {}

            hidden = (lambda k, t: y_hi[:, k % 8, t * P:(t + 1) * P], lambda k, t: y_lo[:, k % 8, t * P:(t + 1) * P])

            def down_groups(*groups):
                m = weights_moving(down, [(base * FG + g, 2 * g, (0, 1)) for g in groups], *hidden,
                                   lambda k: hidden_ready[k // 2], 2, 2 * FG)
                for g in groups:
                    hidden_used[g] = m[NT - 1, 1]
                return m

            for g in range(FG):
                (gate,), gate_done = weights_still(gate_up, base * 2 * FG + g, *h_of, ready, KC, 2)
                s = slice(2 * (g % 4), 2 * (g % 4) + 2)
                tmp = work_v[:, g % 2, :].rearrange("p (a k n) -> p a k n", a=2, k=2)
                pair = lambda i: psum[i][:, :].rearrange("p (k n) -> p k n", k=2)
                act.wait(gate_done, work_v_used[0])
                silu = act.step(partial(nc.scalar.activation, tmp[:, 0], pair(gate), ACT.Silu))
                bank_free[gate] = [silu]
                (up,), up_done = weights_still(gate_up, base * 2 * FG + FG + g, *h_of, ready, KC, 2)
                dve.wait(silu, up_done)
                full = dve.step(partial(nc.vector.tensor_tensor, tmp[:, 1], pair(up), tmp[:, 0], ALU.mult))
                bank_free[up] = [full]
                act.wait(full, hidden_used.get(g - 4), y_used[0])
                hi = act.step(partial(nc.scalar.activation, y_hi[:, s, :], tmp[:, 1], ACT.Copy))
                dve.wait(hi, full)
                lo = dve.step(partial(nc.vector.tensor_tensor, 
                    y_lo[:, s, :], tmp[:, 1], y_hi[:, s, :].bitcast(F32), ALU.subtract))
                hidden_ready[g] = (hi, lo)
                if 0 < g < FG - 1:
                    down_groups(g - 1)
                if g in meanwhile:
                    meanwhile[g]()
            h_used[0] = up_done
            m = down_groups(FG - 2, FG - 1)
            y_used[0] = m[NT - 1, 1]
            work_v_used[0] = lo
            return m

        prob_turn, prob_t_turn = [0], [0]
        prob_free, prob_t_free = [None] * 4, [None] * 2
        W0, W1 = slice(0, P), slice(P, 3 * P)

        def exp_sum(b, top):
            z, s = prob[b], soft[:, b, :]
            act.wait(top)
            for t, w in enumerate((W0, W1)):
                ex = act.step(partial(nc.scalar.activation, z[:, w], z[:, w], ACT.Exp, bias=s[:, t:t + 1],
                                      accum_out=s[:, 2 + t:3 + t]))
            dve.wait(ex)
            return dve.step(partial(nc.vector.reciprocal, s[:, 4:6], s[:, 2:4]))

        def next_prob(score_done):
            b = prob_turn[0] % 4
            prob_turn[0] += 1
            dve.wait(score_done, prob_free[b])
            return b

        def softmax_decayed(i, score_done, h):
            b = next_prob(score_done)
            z, s = prob[b], soft[:, b, :]
            for t, w in enumerate((W0, W1)):
                last = dve.step(partial(
                    nc.vector.scalar_tensor_tensor, out=z[:, w], in0=psum[i][:, w], scalar=c_q[:, t * H + h:t * H + h + 1],
                    in1=mask[:, P:S] if t == 0 else mask, op0=ALU.add, op1=ALU.add))
            bank_free[i] = [last]
            dve.wait(last)
            for t, w in enumerate((W0, W1)):
                top = dve.step(partial(nc.vector.tensor_reduce, s[:, t:t + 1], z[:, w], AX_X, ALU.max, negate=True))
            return b, exp_sum(b, top)

        def softmax_biased(i, score_done, head_bias):
            b = next_prob(score_done)
            z, s = prob[b], soft[:, b, :]
            for t, w in enumerate((W0, W1)):
                last = dve.step(partial(
                    nc.vector.tensor_tensor_reduce, out=z[:, w], in0=psum[i][:, w], in1=head_bias[:, P:S] if t == 0 else head_bias,
                    scale=1.0, scalar=-3e38, op0=ALU.add, op1=ALU.max, accum_out=s[:, 6 + t:7 + t]))
            bank_free[i] = [last]
            dve.wait(last)
            top = dve.step(partial(nc.vector.tensor_scalar, s[:, 0:2], s[:, 6:8], -1.0, None, ALU.mult))
            return b, exp_sum(b, top)

        def scale_prob(b, inv):
            z, s = prob[b], soft[:, b, :]
            dve.wait(inv)
            for t, w in enumerate((W0, W1)):
                last = dve.step(partial(nc.vector.tensor_scalar, z[:, w], z[:, w], s[:, 4 + t:5 + t], None, ALU.mult))
            return last

        def turn_psum(b, ready):
            z = prob[b]
            i = take_bank()
            pe.wait(ready)
            for c in range(3):
                issue = partial(nc.tensor.transpose, psum[i][:, c * P:(c + 1) * P], z[:, c * P:(c + 1) * P], ident)
                turned = pe.step(issue) if c == 2 else pe.do(issue)
            prob_free[b] = turned
            return i, turned

        def turn_prob(b, ready):
            i, turned = turn_psum(b, ready)
            u = prob_t_turn[0] % 2
            prob_t_turn[0] += 1
            act.wait(turned, prob_t_free[u])
            copied = act.step(partial(nc.scalar.activation, prob_t[u][:, :], psum[i][:, 0:3 * P], ACT.Copy))
            bank_free[i] = [copied]
            return u, copied

        def scores(q, k, more=None):
            i = take_bank()
            for t, w in enumerate((W0, W1)):
                o = psum[i][:, w]
                issue = partial(nc.tensor.matmul, 
                    o, q[:, t * P:(t + 1) * P], k[:, 0:(t + 1) * P], start=True, stop=more is None)
                if more is None:
                    m = pe.step(issue)
                else:
                    pe.do(issue)
                    m = more(i, t)
            return i, m

        def token_values(name, blocks, ready, after=lambda n: None):
            done = values_done
            done.clear()
            for c in range(blocks):
                for half in range(2):
                    m = weights_moving(name, [(2 * c + half, half * KC // 2, (c,))], *h_tok, ready, KC // 2, KC)
                    if half:
                        for t in range(NT):
                            act.wait(m[t, c], work_v_used[0])
                            i = 4 + 2 * t + c
                            done.append(act.step(partial(
                                nc.scalar.activation, work_v[:, t, c * 512:(c + 1) * 512], psum[i][:, :], ACT.Copy)))
                            bank_free[i] = [done[-1]]
                    after(2 * c + half)
            return done

        values_done = []

        act.wait(cols_loaded)
        c_ready = act.step(partial(nc.scalar.activation, c_act[:, :], col("c"), ACT.Silu))
        load_next()
        const_loaded = sync.dma(partial(nc.sync.dma_start, const[:, :], dram["const"]), const_in)
        wf_loaded = sync.dma(partial(nc.sync.dma_start, wf_raw[:, :], dram["wf"]), wf_in)
        for _ in range(N_RAW - 1):
            load_next()

        ready = pre_norm([[x_loaded[t]] * 2 for t in range(NT)], col("mix_pre"), None, [cols_loaded], split_next)
        act.wait(wf_loaded)
        wf_rounded = act.step(partial(nc.scalar.activation, wf_hi[:, :], wf_raw[:, :], ACT.Copy))
        dve.wait(wf_rounded)
        wf_rest = dve.step(partial(nc.vector.tensor_tensor, wf_lo[:, :], wf_raw[:, :], wf_hi[:, :].bitcast(F32), ALU.subtract))
        token_values("v1", 1, ready)

        qT = work_b[:, 0:AC, :]
        kT = work_b[:, AC:2 * AC, :]
        qk_ready = {}
        heads1 = []

        def scores_first(h):
            q0 = (h % 2) * HD1
            part = slice(q0, q0 + HD1)
            pe.wait(*qk_ready[h // 4], logf_ready)

            def minus_c(i, t):
                for c in range(t + 1):
                    o = psum[i][:, t * P + c * P:t * P + (t + 1) * P]
                    a = nlogf[:, c * H + h:c * H + h + 1].to_broadcast([P, P])
                    b = tri[c][:, c * P:(t + 1) * P]
                    issue = partial(nc.tensor.matmul, o, a, b, start=False, stop=c == t)
                    m = pe.step(issue) if c == t else pe.do(issue)
                return m

            i, m = scores(qT[part, h // 2, :], kT[part, h // 2, :], minus_c)
            heads1.append((h, i, m))

        attend_bank, turned_first = {}, []

        def finish_first():
            h, i, m = heads1.pop(0)
            dve.wait(cq_ready)
            b, inv = softmax_decayed(i, m, h)
            p_ready = scale_prob(b, inv)
            return h, b, p_ready

        def turn_first(h, b, p_ready):
            turned_first.append((h, *turn_prob(b, p_ready)))

        def values_first(h, u, copied):
            rows = slice((h % 2) * HD1, (h % 2 + 1) * HD1)
            if h % 2 == 0:
                attend_bank[0] = take_bank()
            i = attend_bank[0]
            pe.wait(copied, *values_done)
            o = psum[i]
            v = lambda c: work_v[:, c, h * HD1:(h + 1) * HD1]
            pe.do(partial(nc.tensor.matmul, o[rows, 0:S], v(0), prob_t[u][:, 0:S], start=True, stop=False))
            m = pe.step(partial(nc.tensor.matmul, o[rows, P:S], v(1), prob_t[u][:, S:3 * P], start=False, stop=True))
            prob_t_free[u] = m
            if h % 2 == 1:
                split_bank(i, o[:, 0:S], h // 2, m, y_used[0])
            return m

        y_ready = {}

        def split_bank(i, src, k, done, free, scale=None):
            act.wait(done, free)
            if scale is None:
                hi = act.step(partial(nc.scalar.activation, y_hi[:, k, :], src, ACT.Copy))
                dve.wait(hi, done)
                lo = dve.step(partial(nc.vector.tensor_tensor, y_lo[:, k, :], src, y_hi[:, k, :].bitcast(F32), ALU.subtract))
            else:
                hi = act.step(partial(nc.scalar.activation, y_hi[:, k, :], src, ACT.Copy, scale=scale))
                dve.wait(hi, done)
                lo = dve.step(partial(nc.vector.scalar_tensor_tensor, 
                    out=y_lo[:, k, :], in0=src, scalar=scale, in1=y_hi[:, k, :].bitcast(F32), op0=ALU.mult, op1=ALU.subtract))
            y_ready[k] = (hi, lo)
            bank_free[i] = [hi, lo]

        pair = lambda i: psum[i][:, :].rearrange("p (k n) -> p k n", k=2)
        waiting = []

        def attend_first(n):
            if 0 <= n - 3 < H:
                values_first(*turned_first.pop(0))
            if 0 <= n - 2 < H:
                turn_first(*waiting.pop(0))
            if n < H:
                scores_first(n)
                waiting.append(finish_first())

        def first_qk(g, keys):
            (i,), m = weights_still("qk1", 2 * keys + g, *h_of, ready, KC, 2)
            if keys:
                dve.wait(m)
                k = dve.step(partial(nc.vector.tensor_copy, kT[:, 2 * g:2 * g + 2, :], pair(i)))
            else:
                act.wait(m, *ready(KC - 1))
                k = act.step(partial(nc.scalar.activation, qT[:, 2 * g:2 * g + 2, :], pair(i), ACT.Copy, scale=HD1 ** -0.5))
            bank_free[i] = [k]
            qk_ready[g] = qk_ready.get(g, ()) + (k,)

        first_qk(0, 0)
        fb = take_bank()
        pe.wait(wf_rest)
        for t in range(NT):
            o = psum[fb][:, t * H:(t + 1) * H]
            for k in range(KC):
                a, b = h_tok[0](k, t), h_tok[1](k, t)
                vh, vl = wf_hi[:, k * H:(k + 1) * H], wf_lo[:, k * H:(k + 1) * H]
                pe.do(partial(nc.tensor.matmul, o, a, vh, start=k == 0, stop=False))
                pe.do(partial(nc.tensor.matmul, o, a, vl, start=False, stop=False))
                f_done = pe.step(partial(nc.tensor.matmul, o, b, vh, start=False, stop=k == KC - 1))
        u, a, l, logf, nlogf = (gate_f[:, i, :] for i in range(5))
        dve.wait(f_done, cols_loaded)
        m = dve.step(partial(nc.vector.tensor_tensor, u, psum[fb][:, 0:NT * H], col("b_f"), ALU.add))
        bank_free[fb] = [m]
        act.wait(m)
        m = act.step(partial(nc.scalar.activation, a, u, ACT.Abs))
        act.wait(m)
        m = act.step(partial(nc.scalar.activation, a, a, ACT.Exp, scale=-1.0))
        dve.wait(m)
        m = dve.step(partial(nc.vector.tensor_scalar, a, a, 1.0, None, ALU.add))
        act.wait(m)
        m = act.step(partial(nc.scalar.activation, l, a, ACT.Ln))
        dve.wait(m)
        m = dve.step(partial(nc.vector.scalar_tensor_tensor, out=logf, in0=u, scalar=0.0, in1=l, op0=ALU.min, op1=ALU.subtract))
        dve.wait(m)
        logf_ready = dve.step(partial(nc.vector.tensor_scalar, nlogf, logf, -1.0, None, ALU.mult))

        l0 = COLUMNS["lam"][0]
        quarter = lambda n: cols[:, l0 + n * DIFF:l0 + (n + 1) * DIFF]
        for n in range(2):
            m = dve.step(partial(nc.vector.tensor_tensor, 
                lam_pr[:, n * DIFF:(n + 1) * DIFF], quarter(2 * n), quarter(2 * n + 1), ALU.mult))
        dve.wait(m)
        m = dve.step(partial(nc.vector.tensor_reduce, 
            lam_sb[:, 0:2], lam_pr[:, :].rearrange("p (a n) -> p a n", a=2), AX_X, ALU.add))
        act.wait(m)
        m = act.step(partial(nc.scalar.activation, lam_sb[:, 0:2], lam_sb[:, 0:2], ACT.Exp))
        dve.wait(m)
        m = dve.step(partial(nc.vector.scalar_tensor_tensor, 
            out=lam_sb[:, 2:3], in0=lam_sb[:, 0:1], scalar=LAMBDA_INIT, in1=lam_sb[:, 1:2], op0=ALU.add, op1=ALU.subtract))
        lam_ready = m
        dve.do(partial(nc.vector.tensor_scalar, subln_sc[:, :], col("subln"), 1.0 - LAMBDA_INIT, None, ALU.mult))

        first_qk(0, 1)
        cb = take_bank()
        pe.wait(logf_ready, const_loaded)
        for t in range(NT):
            o = psum[cb][:, t * H:(t + 1) * H]
            for c in range(t + 1):
                a, b = tri[c][:, t * P:(t + 1) * P], logf[:, c * H:(c + 1) * H]
                m = pe.step(partial(nc.tensor.matmul, o, a, b, start=c == 0, stop=c == t))
        dve.wait(m)
        cq_ready = dve.step(partial(nc.vector.tensor_copy, c_q[:, :], psum[cb][:, 0:NT * H]))
        bank_free[cb] = [cq_ready]

        first_qk(1, 0)
        attend_first(0)
        first_qk(1, 1)
        attend_first(1)
        load_gain(0, dram["mix_post"][0])
        load_gain(1, dram["ffn_post"][0])
        load_gain(2, dram["norm_g"][0, 1])

        zc = bias[:, 0:AC, :]
        ya = bias[:, AC:2 * AC, :]
        conv_free = None
        for g in range(2):
            two = slice(2 * g, 2 * g + 2)
            (i,), m = weights_still("mix", 2 + g, *h_of, ready, KC, 2)
            act.wait(m)
            a = act.step(partial(nc.scalar.activation, zc[:, two, :], pair(i), ACT.Copy))
            bank_free[i] = [a]
            attend_first(2 * g + 2)
            (i,), m = weights_still("mix", 4 + g, *h_of, ready, KC, 2)
            dve.wait(m, a)
            z_ready = dve.step(partial(nc.vector.tensor_tensor, zc[:, two, :], pair(i), zc[:, two, :], ALU.mult))
            bank_free[i] = [z_ready]
            attend_first(2 * g + 3)
            for j in range(2 * g, 2 * g + 2):
                tap = lambda n, j=j: col("conv", 3 * j + n, 1)
                act.wait(z_ready)
                m = act.step(partial(nc.scalar.activation, ya[:, j, :], zc[:, j, :], ACT.Copy, scale=tap(2)))
                for shift in (1, 2):
                    dve.wait(m)
                    m = dve.step(partial(nc.vector.scalar_tensor_tensor, 
                        out=ya[:, j, shift:S], in0=zc[:, j, 0:S - shift], scalar=tap(2 - shift), in1=ya[:, j, shift:S],
                        op0=ALU.mult, op1=ALU.add))
        conv_done = m
        conv_ready = {}
        for g in range(2):
            two = slice(2 * g, 2 * g + 2)
            to = slice(AC + 2 * g, AC + 2 * g + 2)
            (i,), m = weights_still("mix", g, *h_of, ready, KC, 2)
            dve.wait(m, conv_done)
            full = dve.step(partial(nc.vector.tensor_tensor, ya[:, two, :], pair(i), ya[:, two, :], ALU.mult))
            bank_free[i] = [full]
            act.wait(full, y_used[0])
            hi = act.step(partial(nc.scalar.activation, y_hi[:, to, :], ya[:, two, :], ACT.Copy))
            dve.wait(hi, full)
            lo = dve.step(partial(nc.vector.tensor_tensor, 
                y_lo[:, to, :], ya[:, two, :], y_hi[:, to, :].bitcast(F32), ALU.subtract))
            conv_free = lo
            for k in (2 * g, 2 * g + 1):
                conv_ready[k] = (hi, lo)
            attend_first(6 + g)

        gate_c = work_a[:, :].rearrange("p (k n) -> p k n", k=KC)
        gate_a = bias
        gate_ready = {}
        for n, place in enumerate((gate_c, gate_a)):
            for g in range(4):
                (i,), m = weights_still("mix", 6 + 4 * n + g, *h_of, ready, KC, 2)
                act.wait(m, conv_free)
                s = act.step(partial(nc.scalar.activation, 
                    place[:, 2 * g:2 * g + 2, :], pair(i), ACT.Sigmoid))
                bank_free[i] = [s]
                gate_ready[n, g] = s
                if n == 0 and g < 3:
                    attend_first(H + g)
        h_used[0] = m

        conv_of = (lambda k: y_hi[:, AC + k, :], lambda k: y_lo[:, AC + k, :])
        attn_of = (lambda k: y_hi[:, k, :], lambda k: y_lo[:, k, :])
        merged = {}
        conv_part = {}
        for n in range(2):
            for half in range(2):
                src, rdy = (conv_of, lambda k: conv_ready[k]) if n == 0 else (attn_of, lambda k: y_ready[k])
                banks, m = weights_still("branch", 2 * n + half, *src, rdy, AC, 4)
                for b, i in enumerate(banks):
                    g = 2 * half + b
                    two = slice(2 * g, 2 * g + 2)
                    place = gate_c if n == 0 else gate_a
                    dve.wait(m, gate_ready[n, g])
                    full = dve.step(partial(nc.vector.tensor_tensor, 
                        place[:, two, :], pair(i), place[:, two, :], ALU.mult))
                    bank_free[i] = [full]
                    if n == 0:
                        conv_part[g] = full
                        continue
                    dve.wait(full, conv_part[g])
                    full = dve.step(partial(nc.vector.tensor_tensor, 
                        gate_a[:, two, :], gate_a[:, two, :], gate_c[:, two, :], ALU.add))
                    act.wait(full, h_used[0])
                    hi = act.step(partial(nc.scalar.activation, h_hi[:, two, :], gate_a[:, two, :], ACT.Copy))
                    dve.wait(hi, full)
                    lo = dve.step(partial(nc.vector.tensor_tensor, 
                        h_lo[:, two, :], gate_a[:, two, :], h_hi[:, two, :].bitcast(F32), ALU.subtract))
                    for k in (2 * g, 2 * g + 1):
                        merged[k] = (hi, lo)
        y_used[0] = m
        work_used[0] = full
        work_v_used[0] = m

        def wide_product(name, order, tok, rdy, between=()):
            part = lambda index: (index, index % 2 * KC // 2, (index // 2,))
            for n, index in enumerate(order[:2]):
                weights_moving(name, [part(index)], *tok, rdy, KC // 2, KC)
                for work in between[n:n + 1]:
                    work()
            return weights_moving(name, [part(index) for index in order[2:]], *tok, rdy, KC // 2, KC)

        marks = wide_product("out1", (0, 2, 1, 3), h_tok, lambda k: merged[k])
        h_used[0] = marks[NT - 1, 1]
        x_ready = post_norm(marks, 0)
        load_gain(0, dram["norm_g"][0, 3])
        ready = pre_norm(x_ready, col("ffn_pre"), None, [])

        table, hot = prob[0][0:BUCKETS + 1, 0:H], prob[1][0:BUCKETS + 1, :]
        bias_ready, diagonal_in = [], []
        bias_given = [prob_free[0], prob_free[1], work_used[0]]

        def load_table():
            pool.wait(*bias_given)
            pool.dma(partial(nc.gpsimd.dma_start, table, dram["rel_table"]), table_in)
            bias_given.append(pool.dma(partial(nc.gpsimd.dma_start, hot, dram["bucket_of"]), table_in))

        def spread_table():
            i = take_bank()
            pe.wait(bias_given[-1])
            m = pe.step(partial(nc.tensor.matmul, psum[i][0:H, 0:BIAS_W], table, hot, start=True, stop=True))
            dve.wait(m, prob_free[2])
            rows = dve.step(partial(nc.vector.tensor_copy, prob[2][0:H, :], psum[i][0:H, 0:BIAS_W]))
            bank_free[i] = [rows]
            pool.wait(rows)
            kept = pool.dma(partial(nc.gpsimd.dma_start, bias_dram, prob[2][0:H, :]), bias_sig)
            pool.wait(kept)
            diagonal = bass.AP(bias_dram.tensor, 0, [[1, P], [BIAS_W, H], [1, S]])
            diagonal_in.append(pool.dma(partial(nc.gpsimd.dma_start, bias[:, :, :], diagonal), bias_sig))
            prob_free[0] = prob_free[1] = m
            prob_free[2] = kept

        def flip_bias():
            pe.wait(diagonal_in[0])
            for h in range(0, H, 2):
                i = take_bank()
                two = bias[:, h:h + 2, :]
                flipped = pe.step(partial(nc.tensor.matmul, pair(i), flip, two, start=True, stop=True))
                dve.wait(flipped)
                bias_ready.append(dve.step(partial(nc.vector.tensor_copy, two, pair(i))))
                bank_free[i] = [bias_ready[-1]]

        marks = feed_forward("gate_up1", "down1", 0, ready, {0: load_table, 2: spread_table, 5: flip_bias})
        x_ready = post_norm(marks, 1)
        load_gain(1, dram["norm_g"][1, 1])

        for layer, name in enumerate(("moba", "diff")):
            q_scale = (HD2 if layer == 0 else DIFF) ** -0.5
            scale, shift = mod_cols[:, 4 * layer, :], mod_cols[:, 4 * layer + 1, :]
            ready = pre_norm(x_ready, scale, shift, [mod_ready[layer, 0, 0], mod_ready[layer, 0, 1]])
            heads = work[:, :].rearrange("p (h n) -> p h n", h=H)
            qk_ready, softened, turned_heads, diff_squares = {}, {}, {}, {}
            y_ready.clear()

            def score_head(h):
                pe.wait(*qk_ready[h // 2])
                halves = 1 if layer == 0 else 2
                width = P // halves
                got = []
                for c in range(halves):
                    part = slice(c * width, (c + 1) * width)
                    i, m = scores(heads[part, h, 0:S], heads[part, h, S:2 * S])
                    dve.wait(bias_ready[-1])
                    got.append(softmax_biased(i, m, bias[:, h, :]))
                b, inv = got[0]
                last = scale_prob(b, inv)
                if layer == 1:
                    b2, inv2 = got[1]
                    s2 = soft[:, b2, :]
                    dve.wait(inv2, lam_ready)
                    m2 = dve.step(partial(nc.vector.tensor_scalar, s2[:, 4:6], s2[:, 4:6], lam_sb[:, 2:3], -1.0, ALU.mult, ALU.mult))
                    dve.wait(m2, last)
                    for t, w in enumerate((W0, W1)):
                        last = dve.step(partial(
                            nc.vector.scalar_tensor_tensor, out=prob[b][:, w], in0=prob[b2][:, w],
                            scalar=s2[:, 4 + t:5 + t], in1=prob[b][:, w], op0=ALU.mult, op1=ALU.add))
                    prob_free[b2] = last
                softened[h] = (b, last)

            def turn_head(h):
                b, p_ready = softened[h]
                i, turned = turn_psum(b, p_ready)
                act.wait(turned)
                copied = act.step(partial(nc.scalar.activation, heads[:, h, 0:3 * P], psum[i][:, 0:3 * P], ACT.Copy))
                bank_free[i] = [copied]
                turned_heads[h] = copied

            def apply_head(h, values_done):
                i = take_bank()
                pe.wait(turned_heads[h], *values_done)
                v = lambda c: work_v[:, c, h * P:(h + 1) * P]
                o, pt = psum[i], heads[:, h, :]
                if layer == 0:
                    pe.do(partial(nc.tensor.matmul, o[:, 0:S], v(0), pt[:, 0:S], start=True, stop=False))
                    m = pe.step(partial(nc.tensor.matmul, o[:, P:S], v(1), pt[:, S:3 * P], start=False, stop=True))
                    split_bank(i, o[:, 0:S], h, m, y_used[0])
                    return m
                pe.do(partial(nc.tensor.matmul, o[:, 0:P], pt[:, 0:P], v(0), start=True, stop=True))
                pe.do(partial(nc.tensor.matmul, o[:, P:S], pt[:, P:S], v(0), start=True, stop=False))
                m = pe.step(partial(nc.tensor.matmul, o[:, P:S], pt[:, S:3 * P], v(1), start=False, stop=True))
                dve.wait(m)
                o_copied = dve.step(partial(nc.vector.tensor_copy, pt[:, 0:S], o[:, 0:S]))
                bank_free[i] = [o_copied]
                act.wait(o_copied, square_free[0])
                for t in range(NT):
                    sq = act.step(partial(
                        nc.scalar.activation, lam_pr[:, :], pt[:, t * P:(t + 1) * P], ACT.Square,
                        accum_out=diff_stat[:, NT * h + t:NT * h + t + 1]))
                    act.wait(sq)
                square_free[0] = sq
                diff_squares[h] = sq
                return m

            square_free = [lam_ready]

            def head_rms(hs):
                n = NT * len(hs)
                sums = diff_stat[:, NT * hs[0]:NT * hs[0] + n]
                dve.wait(diff_squares[hs[-1]])
                m = dve.step(partial(nc.vector.tensor_scalar, sums, sums, 1.0 / HD2, EPS, ALU.mult, ALU.add))
                return inverse_rms(sums, n, m)

            def norm_heads(hs, r):
                dve.wait(r)
                scaled = {}
                for h in hs:
                    for t in range(NT):
                        w = heads[:, h, t * P:(t + 1) * P]
                        scaled[h] = dve.step(partial(
                            nc.vector.tensor_scalar, w, w, diff_stat[:, NT * h + t:NT * h + t + 1], None, ALU.mult))
                for h in hs:
                    i = take_bank()
                    pe.wait(scaled[h])
                    for t in range(NT):
                        m = pe.step(partial(nc.tensor.transpose, psum[i][:, t * P:(t + 1) * P], heads[:, h, t * P:(t + 1) * P], ident))
                    split_bank(i, psum[i][:, 0:S], h, m, y_used[0], scale=subln_sc[:, 0:1])
                return m

            def attend(n):
                if 0 <= n - 2 < H:
                    turn_head(n - 2)
                if 0 <= n < H:
                    score_head(n)

            for g in range(4):
                two = slice(2 * g, 2 * g + 2)
                (i,), m = weights_still(name + "_qk", g, *h_of, ready, KC, 2)
                act.wait(m, work_used[0])
                q = act.step(partial(nc.scalar.activation, heads[:, two, 0:S], pair(i), ACT.Copy, scale=q_scale))
                bank_free[i] = [q]
                attend(2 * g - 2)
                (i,), m = weights_still(name + "_qk", 4 + g, *h_of, ready, KC, 2)
                act.wait(m)
                k = act.step(partial(nc.scalar.activation, heads[:, two, S:2 * S], pair(i), ACT.Copy))
                bank_free[i] = [k]
                qk_ready[g] = (q, k)
                attend(2 * g - 1)

            rms = []

            def after_values(n):
                attend(H - 2 + n)
                if n == 2:
                    for h in range(4):
                        apply_head(h, values_done)
                    if layer == 1:
                        rms.append(head_rms(range(4)))

            def late_values():
                for h in range(4, H):
                    last_read[0] = apply_head(h, values_done)
                if layer == 1:
                    rms.append(head_rms(range(4, H)))

            def late_norm():
                if layer == 1:
                    last_read[0] = norm_heads(range(4, H), rms[1])

            last_read = [None]
            token_values(name + "_v", 2, ready, after_values)
            h_used[0] = values_done[-1]
            if layer == 1:
                norm_heads(range(4), rms[0])
            marks = wide_product(name + "_o", (0, 2, 1, 3), y_tok, lambda k: y_ready[k], [late_values, late_norm])
            work_v_used[0] = work_used[0] = last_read[0]
            y_used[0] = marks[NT - 1, 1]
            slot = gain_slot[layer, 0]
            x_ready = post_norm(marks, slot)
            if layer == 0:
                load_gain(slot, dram["norm_g"][1, 3])
            scale, shift = mod_cols[:, 4 * layer + 2, :], mod_cols[:, 4 * layer + 3, :]
            ready = pre_norm(x_ready, scale, shift, [mod_ready[layer, 1, 0], mod_ready[layer, 1, 1]])
            marks = feed_forward("gate_up2", "down2", layer, ready)
            x_ready = post_norm(marks, gain_slot[layer, 1])

        for t in range(NT):
            sync.wait(*x_ready[t])
            done = sync.dma(partial(nc.sync.dma_start, out[t * P:(t + 1) * P, :], x_res[:, t, :]), stored)
        sync.wait(done)

        block = ctx.enter_context(nc.Block())

        @block.sync
        def _(e):
            sync.play(e)

        @block.scalar
        def _(e):
            act.play(e)

        @block.vector
        def _(e):
            dve.play(e)

        @block.gpsimd
        def _(e):
            pool.play(e)

        @block.tensor
        def _(e):
            pe.play(e)


def kernel(**inputs):
    import numpy as np
    import concourse.bacc as bacc
    from concourse.bass_utils import run_bass_kernel_spmd as run

    a = {name: np.asarray(value) for name, value in inputs.items()}
    put = np.ascontiguousarray

    def slabs(w, kcs, width):
        K, N = w.shape
        return put(w.reshape(K // (P * kcs), kcs, P, N // width, width).transpose(3, 0, 2, 1, 4)).reshape(-1, P, kcs * width)

    def columns(v):
        return v.reshape(-1, P).T

    w_in = a["w_in"][0]
    rest = 3 * AW + H
    qkv = {"moba": a["moba_w_qkv_2"][0], "diff": a["diff_w_qkv_2"][0]}
    rel = (BIAS_W - P - 1) - np.arange(BIAS_W)
    n = np.maximum(rel, 1).astype(np.float32)
    half = BUCKETS // 2
    far = half + (np.log(n / half) / math.log(2048 / half) * (BUCKETS - half)).astype(np.int32)
    bucket = np.where(rel < half, rel, np.minimum(far, BUCKETS - 1))
    bucket = np.where(rel < 0, BUCKETS, bucket)
    bucket_of = (bucket[None, :] == np.arange(BUCKETS + 1)[:, None]).astype(np.float32)
    const = np.zeros((P, N_CONST), np.float32)
    row, s = np.arange(P)[:, None], np.arange(S)[None, :]
    const[:, IDENT:IDENT + P] = np.eye(P)
    const[:, ONES:ONES + P] = 1.0
    const[:, FLIP:FLIP + P] = np.eye(P)[::-1]
    for c in range(NT):
        const[:, TRI + c * S:TRI + (c + 1) * S] = c * P + row <= s
    const[:, MASK:MASK + S] = np.where(s > row + P, NEG, 0.0)
    small = {
        "mix_pre": columns(a["norm_mix_pre"][0]), "ffn_pre": columns(a["norm_ffn_pre"][0]), "c": columns(a["c_2"][0]),
        "g00": columns(a["norm_g_2"][0, 0]), "g02": columns(a["norm_g_2"][0, 2]),
        "g10": columns(a["norm_g_2"][1, 0]), "g12": columns(a["norm_g_2"][1, 2]),
        "conv": a["conv_w"][0].reshape(3, AC, P).transpose(2, 1, 0).reshape(P, 3 * AC),
        "subln": columns(a["diff_subln_g_2"][0]),
        "b_f": np.broadcast_to(np.concatenate([a["b_f"][0]] * NT)[None, :], (P, NT * H)),
        "lam": np.broadcast_to(a["diff_lambda_2"][0].reshape(1, -1), (P, 4 * DIFF)),
    }
    arrays = {
        "x": a["x"][0],
        "cols": np.concatenate([small[k] for k in COLUMNS], axis=1),
        "const": const,
        "bucket_of": bucket_of,
        "rel_table": np.concatenate([a["rel_bias_2"], np.full((1, H), NEG, np.float32)], axis=0),
        "wf": w_in[:, 3 * AW:rest].reshape(KC, P, H).transpose(1, 0, 2).reshape(P, KC * H),
        "qk1": slabs(w_in[:, 0:2 * AW], KC, 256),
        "v1": slabs(w_in[:, 2 * AW:3 * AW], KC // 2, 512),
        "mix": slabs(w_in[:, rest:], KC, 256),
        "branch": np.concatenate([slabs(a["w_branch"][0, i], AC, 512) for i in range(2)]),
        "out1": slabs(a["w_out"][0], KC // 2, 512),
        "gate_up1": slabs(a["w_gate_up"][0], KC, 256),
        "down1": slabs(a["w_down"][0], 2, D),
        "gate_up2": np.concatenate([slabs(a["ffn_w_in_2"][i], KC, 256) for i in range(2)]),
        "down2": np.concatenate([slabs(a["ffn_w_out_2"][i], 2, D) for i in range(2)]),
        "ada": np.concatenate([slabs(a["ada_w_2"][i], 1, SLAB) for i in range(2)]),
        "ada_b": a["ada_b_2"].reshape(-1, SLAB),
        "mix_post": a["norm_mix_post"], "ffn_post": a["norm_ffn_post"], "norm_g": a["norm_g_2"],
    }
    for name, w in qkv.items():
        arrays[name + "_qk"] = slabs(w[:, 0:2 * D], KC, 256)
        arrays[name + "_v"] = slabs(w[:, 2 * D:], KC // 2, 512)
        arrays[name + "_o"] = slabs(a[name + "_w_o_2"][0], KC // 2, 512)

    nc = bacc.Bacc("TRN2", target_bir_lowering=False, num_devices=1, dynamic_dma_scratch_size=2048)
    arrays = {"in_" + k: put(v) for k, v in arrays.items()}
    dram = {k[3:]: nc.dram_tensor(k, v.shape, mybir.dt.from_np(v.dtype), kind="ExternalInput").ap() for k, v in arrays.items()}
    out = nc.dram_tensor("out", (S, D), F32, kind="ExternalOutput").ap()
    build_program(nc, dram, out)
    result = run(nc, [arrays], core_ids=[0])
    return result.results[0]["out"].reshape(1, S, D)
```

```python
import math
from contextlib import ExitStack
from functools import partial

import concourse.bass as bass
from concourse import mybir

F32 = mybir.dt.float32
F32R = mybir.dt.float32r
ALU = mybir.AluOpType
ACT = mybir.ActivationFunctionType
AX_X = mybir.AxisListType.X

P = 128
S = 256
NT = S // P
D = 1024
KC = D // P
H = 8
HD1 = 64
AW = H * HD1
AC = AW // P
HD2 = D // H
DIFF = HD2 // 2
FF = -(-8 * D // (3 * 256)) * 256
FG = FF // 256
BUCKETS = 32
EPS = 1e-6
NEG = -1e30
LAMBDA_INIT = 0.8 - 0.6 * math.exp(-0.3 * 1)

SLAB = 2048
N_RAW, N_HI, N_LO = 6, 4, 4
AHEAD = 3

COLUMNS = {}
for _name, _n in (("mix_pre", KC), ("ffn_pre", KC), ("c", KC), ("g00", KC), ("g02", KC), ("g10", KC), ("g12", KC),
                  ("conv", 3 * AC), ("subln", 1), ("b_f", NT * H), ("lam", 4 * DIFF)):
    COLUMNS[_name] = (sum(w for _, w in COLUMNS.values()), _n)
N_COLUMNS = sum(w for _, w in COLUMNS.values())

IDENT, FLIP, TRI, ONES = 0, P, 2 * P, 3 * P
MASK = ONES + P
N_CONST = MASK + S
BIAS_W = 3 * P


class Mark:

    def __init__(self, sem, value):
        self.sem, self.value = sem, value


class Counter:

    def __init__(self, sem):
        self.sem, self.count = sem, 0

    def step(self, n):
        self.count += n
        return Mark(self.sem, self.count)


class Queue:

    def __init__(self, counter):
        self.counter, self.items, self.seen = counter, [], {}

    def wait(self, *marks):
        for m in marks:
            if m is not None and self.seen.get(id(m.sem), 0) < m.value:
                self.seen[id(m.sem)] = m.value
                self.items.append((None, m.sem, m.value))

    def do(self, issue):
        self.items.append((issue, None, 0))

    def step(self, issue):
        m = self.counter.step(1)
        self.items.append((issue, m.sem, 1))
        return m

    def dma(self, issue, counter):
        m = counter.step(16)
        self.items.append((issue, m.sem, 16))
        return m

    def play(self, engine):
        for issue, sem, n in self.items:
            if issue is None:
                engine.wait_ge(sem, n)
            elif sem is None:
                issue()
            else:
                issue().then_inc(sem, n)


def slab_order():
    def ffn(gate_up, down, base):
        order = []
        for g in range(FG):
            order += [(gate_up, base * 2 * FG + g), (gate_up, base * 2 * FG + FG + g)]
            if g:
                order.append((down, base * FG + g - 1))
        return order + [(down, base * FG + FG - 1)]

    order = [("v1", 0), ("v1", 1)]
    for i in range(2):
        order += [("qk1", i), ("qk1", 2 + i)]
    order += [("mix", 2), ("mix", 4), ("mix", 3), ("mix", 5), ("mix", 0), ("mix", 1)]
    order += [("mix", 6 + i) for i in range(8)]
    order += [("branch", i) for i in range(4)] + [("out1", i) for i in (0, 2, 1, 3)]
    order += ffn("gate_up1", "down1", 0)
    for i, name in enumerate(("moba", "diff")):
        order += [(name + "_v", j) for j in range(2 - 2 * i)]
        for j in range(4):
            order += [(name + "_qk", j), (name + "_qk", 4 + j)]
        order += [(name + "_v", j) for j in range(2 - 2 * i, 4)]
        order += [(name + "_o", j) for j in (0, 2, 1, 3)]
        order += ffn("gate_up2", "down2", i)
    return order


def build_program(nc, dram, out):
    with ExitStack() as ctx:
        def sb(name, shape, dt=F32):
            return ctx.enter_context(nc.sbuf_tensor(name, shape, dt))

        def sem(name):
            return ctx.enter_context(nc.semaphore(name))

        raw = [sb(f"raw{i}", [P, SLAB]) for i in range(N_RAW)]
        high = [sb(f"high{i}", [P, SLAB], F32R) for i in range(N_HI)]
        low = [sb(f"low{i}", [P, SLAB], F32R) for i in range(N_LO)]
        x_res = sb("x_res", [P, NT, D])
        h_hi = sb("h_hi", [P, KC, S], F32R)
        h_lo = sb("h_lo", [P, KC, S], F32R)
        y_hi = sb("y_hi", [P, KC, S], F32R)
        y_lo = sb("y_lo", [P, KC, S], F32R)
        work = sb("work", [P, 2 * NT * D])
        work_a = work[:, 0:NT * D]
        work_b = work[:, NT * D:].rearrange("p (k n) -> p k n", k=KC)
        work_v = sb("work_v", [P, NT, D])
        bias = sb("bias", [P, H, S])
        gain = [sb(f"gain{i}", [P, D]) for i in range(3)]
        ada = sb("ada", [P, SLAB])
        prob = [sb(f"prob{i}", [P, 3 * P]) for i in range(4)]
        prob_t = [sb(f"prob_t{i}", [P, 3 * P]) for i in range(2)]
        const = sb("const", [P, N_CONST])
        cols = sb("cols", [P, N_COLUMNS])
        c_act = sb("c_act", [P, KC])
        mod_cols = sb("mod_cols", [P, 8, KC])
        stat = sb("stat", [P, 32])
        soft = sb("soft", [P, 4, 8])
        lam_sb = sb("lam_sb", [P, 4])
        lam_pr = sb("lam_pr", [P, 2 * DIFF])
        subln_sc = sb("subln_sc", [P, 1])
        wf_raw = sb("wf_raw", [P, KC * H])
        wf_hi = sb("wf_hi", [P, KC * H], F32R)
        wf_lo = sb("wf_lo", [P, KC * H], F32R)
        gate_f = sb("gate_f", [P, 5, NT * H])
        c_q = sb("c_q", [P, NT * H])
        ck_hi = sb("ck_hi", [H, S], F32R)
        ck_lo = sb("ck_lo", [H, S], F32R)
        ident_r = sb("ident_r", [H, H], F32R)
        diff_stat = sb("diff_stat", [P, NT * H])
        psum = [ctx.enter_context(nc.psum_tensor(f"psum{i}", [P, 512], F32)) for i in range(8)]
        bias_dram = nc.dram_tensor("bias_dram", (H, BIAS_W), F32, kind="Internal").ap()

        pe = Queue(Counter(sem("pe_done")))
        act = Queue(Counter(sem("act_done")))
        dve = Queue(Counter(sem("dve_done")))
        pool = Queue(Counter(sem("pool_done")))
        sync = Queue(None)
        raw_in = [Counter(sem(f"raw_in{i}")) for i in range(N_RAW)]
        x_in = [Counter(sem(f"x_in{t}")) for t in range(NT)]
        const_in, cols_in, wf_in = (Counter(sem(n)) for n in ("const_in", "cols_in", "wf_in"))
        bias_sig = Counter(sem("bias_sig"))
        ident_in = Counter(sem("ident_in"))
        table_in = Counter(sem("table_in"))
        ada_in = Counter(sem("ada_in"))
        gain_in = [Counter(sem(f"gain_in{i}")) for i in range(3)]
        stored = Counter(sem("stored"))

        ident = const[:, IDENT:IDENT + P]
        ones = const[:, ONES:ONES + P]
        flip = const[:, FLIP:FLIP + P]
        tri = const[:, TRI:ONES + P]
        mask = const[:, MASK:MASK + S]

        def col(name, a=0, n=None):
            o, w = COLUMNS[name]
            return cols[:, o + a:o + a + (w if n is None else n)]

        x_loaded = [sync.dma(partial(nc.sync.dma_start, x_res[:, t, :], dram["x"][t * P:(t + 1) * P, :]), x_in[t]) for t in range(NT)]
        cols_loaded = act.dma(partial(nc.scalar.dma_start, cols[:, :], dram["cols"]), cols_in)
        ident_loaded = act.dma(partial(nc.scalar.dma_start, ident, dram["const"][:, IDENT:IDENT + P]), ident_in)

        bank_free = [[] for _ in range(8)]
        turn = [0]

        def take_bank():
            i = turn[0] % 4
            turn[0] += 1
            pe.wait(*bank_free[i])
            bank_free[i] = []
            return i

        main = slab_order()
        first_of = {key: main.index(key) for key in (("gate_up1", 0), ("moba_v", 0), ("gate_up2", 0), ("diff_qk", 0))}
        turn5 = main.index(("gate_up2", 2 * FG))
        turn1, turn2, turn3, turn4 = sorted(first_of.values())
        ada_plan = [(1, turn1 - 2, True), (turn1 + 4, turn1 + 15, False), (turn1 + 19, turn2 - 2, True),
                    (turn2 + 4, turn3 - 2, True), (turn3 + 4, turn4 - 2, True), (turn4 + 1, turn5 - 3, True)]
        last_block = len(ada_plan) - 1
        after_main = {}
        for b, (lo, hi, _) in enumerate(ada_plan):
            for k in range(KC):
                at = lo + k * (hi - lo) // (KC - 1) if b else (4 + k if k < 2 else 14 + 2 * (k - 2))
                after_main.setdefault(at, []).append(b * KC + k)
        stream = []
        for m in range(len(main)):
            stream += [("main", m)] + [("ada", n) for n in after_main.get(m, [])]
        raw_free = [None] * N_RAW
        loads = [0]
        raw_loaded = {}

        def load_next():
            i = loads[0]
            if i >= len(stream):
                return
            loads[0] += 1
            kind, n = stream[i]
            src = dram["ada"][n] if kind == "ada" else dram[main[n][0]][main[n][1]]
            slot = i % N_RAW
            sync.wait(raw_free[slot])
            raw_loaded[i] = sync.dma(partial(nc.sync.dma_start, raw[slot][:, :], src), raw_in[slot])

        slab_used = {}
        slab_split = {}
        done_items = [0]
        pending, at_norm = [], []
        ada_state = {"init": None, "free": None}

        def split_slab(i, n, s):
            src, hi, lo = raw[i % N_RAW][:, s], high[n % N_HI][:, s], low[n % N_LO][:, s]
            act.wait(raw_loaded[i], slab_used.get(n - N_HI))
            rounded = act.step(partial(nc.scalar.activation, hi, src, ACT.Copy))
            dve.wait(rounded, slab_used.get(n - N_LO))
            rest = dve.step(partial(nc.vector.tensor_tensor, lo, src, hi.bitcast(F32), ALU.subtract))
            return (rounded, rest), rest

        def split_next():
            i = done_items[0]
            done_items[0] += 1
            kind, n = stream[i]
            slot = i % N_RAW
            src = raw[slot]
            if kind == "main":
                slab_split[n], raw_free[slot] = split_slab(i, n, slice(0, SLAB))
            else:
                block, k = divmod(n, KC)
                if k == 0:
                    assert not pending and not at_norm
                    pool.wait(ada_state["free"])
                    cleared = pool.step(partial(nc.gpsimd.memset, ada[:, :], 0.0))
                    pool.wait(cleared)
                    ada_state["init"] = pool.dma(partial(nc.gpsimd.dma_start, ada[0:1, :], dram["ada_b"][block:block + 1, :]), ada_in)
                dve.wait(raw_loaded[i], ada_state["init"], c_ready)
                summed = dve.step(partial(nc.vector.scalar_tensor_tensor, 
                    out=ada[:, :], in0=src[:, :], scalar=c_act[:, k:k + 1], in1=ada[:, :], op0=ALU.mult, op1=ALU.add))
                ada_state["init"] = summed
                raw_free[slot] = summed
                if k == KC - 1:
                    if block == last_block:
                        pending.append(partial(finish_ada, block, summed, (0,)))
                        at_norm.append(partial(finish_ada, block, summed, (1,)))
                    else:
                        (at_norm if ada_plan[block][2] else pending).append(partial(finish_ada, block, summed))
            load_next()

        used = [0]

        behind_split = []

        def split_up_to(n):
            while n not in slab_split and done_items[0] < len(stream):
                split_next()

        def next_slab(name, index, ahead=AHEAD):
            n = used[0]
            used[0] += 1
            assert main[n] == (name, index), (main[n], name, index)
            split_up_to(n + ahead)
            while behind_split:
                behind_split.pop(0)()
            pe.wait(*slab_split[n])
            return n, high[n % N_HI], low[n % N_LO]

        def slab_done(n, mark):
            slab_used[n] = mark
            while pending:
                for evacuate in pending.pop(0)():
                    evacuate()

        def weights_still(name, index, hi, lo, ready, kcs, n_chunks):
            n, wh, wl = next_slab(name, index)
            wh = wh[:, :].rearrange("p (k n) -> p k n", k=kcs)
            wl = wl[:, :].rearrange("p (k n) -> p k n", k=kcs)
            banks = []
            for j0 in range(0, n_chunks, 2):
                banks.append(take_bank())
                for k in range(kcs):
                    pe.wait(*ready(k))
                    for j in (j0, j0 + 1):
                        o = psum[banks[-1]][:, (j - j0) * S:(j - j0 + 1) * S]
                        a, b = wh[:, k, j * P:(j + 1) * P], wl[:, k, j * P:(j + 1) * P]
                        first, last = k == 0 and j == j0, k == kcs - 1
                        pe.do(partial(nc.tensor.matmul, o, a, hi(k), start=first, stop=False))
                        pe.do(partial(nc.tensor.matmul, o, a, lo(k), start=False, stop=False))
                        issue = partial(nc.tensor.matmul, o, b, hi(k), start=False, stop=last and j > j0)
                        mark = pe.step(issue) if last and j > j0 else pe.do(issue)
            slab_done(n, mark)
            return banks, mark

        def weights_moving(name, parts, hi, lo, ready, kcs, k_all, between={}, hold=0):
            slabs, marks = {}, {}
            order = [(0, i, c) for i, (_, _, blocks) in enumerate(parts) for c in blocks]
            order += sorted(((1, i, c) for _, i, c in order), key=lambda at: at[2])
            for t, i, c in order:
                index, k0, blocks = parts[i]
                if i not in slabs:
                    n, *halves = next_slab(name, index, AHEAD - i - hold)
                    slabs[i] = (n, *(w[:, :].rearrange("p (k n) -> p k n", k=kcs) for w in halves))
                n, wh, wl = slabs[i]
                o, j = psum[4 + 2 * t + c][:, :], blocks.index(c)
                for k in range(kcs):
                    if n == 0 and k == kcs // 2:
                        pe.wait(*second_half)
                    pe.wait(*ready(k0 + k, t))
                    a, b = hi(k0 + k, t), lo(k0 + k, t)
                    vh, vl = wh[:, k, j * 512:(j + 1) * 512], wl[:, k, j * 512:(j + 1) * 512]
                    first, last = k0 + k == 0, k0 + k == k_all - 1
                    if first:
                        pe.wait(*bank_free[4 + 2 * t + c])
                        bank_free[4 + 2 * t + c] = []
                    pe.do(partial(nc.tensor.matmul, o, a, vh, start=first, stop=False))
                    pe.do(partial(nc.tensor.matmul, o, a, vl, start=False, stop=False))
                    issue = partial(nc.tensor.matmul, o, b, vh, start=False, stop=last)
                    if k == kcs - 1:
                        marks[t, c] = pe.step(issue)
                    else:
                        pe.do(issue)
                if t == NT - 1 and c == blocks[-1]:
                    slab_done(n, marks[t, c])
                if (t, i) in between:
                    between[t, i]()
            return marks

        gain_ready = [None] * 3
        gain_used = [None] * 3

        def load_gain(slot, src):
            pool.wait(gain_used[slot])
            gain_used[slot] = None
            gain_ready[slot] = pool.dma(partial(nc.gpsimd.dma_start, gain[slot][:, :], src.partition_broadcast(P)), gain_in[slot])

        gain_slot = {(0, 0): 2, (0, 1): 0, (1, 0): 1, (1, 1): 2}
        mod_ready = {}

        def finish_ada(block, summed, halves=(0, 1), spare=None):
            layer, b = divmod(block, 3)
            evacuations = []

            def next_bank():
                if not spare:
                    return take_bank()
                i = spare.pop(0)
                pe.wait(*bank_free[i])
                bank_free[i] = []
                return i

            def take_column(i, summed, layer, part, what):
                dve.wait(summed)
                place = mod_cols[:, 4 * layer + 2 * part + (1 - what), :]
                if what == 0:
                    got = dve.step(partial(nc.vector.tensor_copy, place, psum[i][:, 0:KC]))
                else:
                    g = col(f"g{layer}{2 * part}")
                    got = dve.step(partial(nc.vector.scalar_tensor_tensor,
                        out=place, in0=psum[i][:, 0:KC], scalar=1.0, in1=g, op0=ALU.add, op1=ALU.mult))
                bank_free[i] = [got]
                mod_ready[layer, part, what] = got

            def take_gain(i, summed, slot, c):
                assert gain_used[slot] is None and gain_ready[slot] is not None
                dve.wait(summed, gain_ready[slot])
                g = gain[slot][:, c * 512:(c + 1) * 512]
                got = dve.step(partial(nc.vector.tensor_tensor, g, psum[i][:, :], g, ALU.mult))
                bank_free[i] = [got]
                if c == 1:
                    gain_ready[slot] = got

            pe.wait(summed)
            for half in halves:
                section = 2 * b + half
                part, what = divmod(section, 3)
                if what < 2:
                    i = next_bank()
                    for k in range(KC):
                        a = ada[:, half * D + k * P:half * D + (k + 1) * P]
                        issue = partial(nc.tensor.matmul, psum[i][:, k:k + 1], a, ones[:, 0:1], start=True, stop=True)
                        last = pe.step(issue) if k == KC - 1 else pe.do(issue)
                    evacuations.append(partial(take_column, i, last, layer, part, what))
                else:
                    for c in range(2):
                        i = next_bank()
                        a = ada[:, half * D + c * 512:half * D + (c + 1) * 512]
                        last = pe.step(partial(nc.tensor.matmul, psum[i][:, :], ones, a, start=True, stop=True))
                        evacuations.append(partial(take_gain, i, last, gain_slot[layer, part], c))
            ada_state["free"] = last
            return evacuations

        minus_half = sb("minus_half", [P, NT * H])
        halves_ready = pool.step(partial(nc.gpsimd.memset, minus_half[:, :], -0.5))

        def inverse_rms(sums, n, given):
            pool.wait(given, halves_ready)
            return pool.step(partial(nc.gpsimd.tensor_tensor, sums, sums, minus_half[:, 0:n], ALU.pow))

        h_used = [None]
        work_used = [None]
        work_v_used = [None]

        def half_of(t, c):
            return slice((2 * t + c) * 512, (2 * t + c + 1) * 512)

        def square_half(src, ready, t, c, base):
            act.wait(ready)
            return act.step(partial(
                nc.scalar.activation, work_v[:, t, c * 512:(c + 1) * 512], src, ACT.Square, scale=D ** -0.5,
                accum_out=stat[:, base + 2 * t + c:base + 2 * t + c + 1]))

        def join_halves(squares, t, base):
            a = stat[:, base + 2 * t:base + 2 * t + 1]
            dve.wait(*squares)
            m = dve.step(partial(nc.vector.scalar_tensor_tensor, out=a, in0=a, scalar=EPS,
                                 in1=stat[:, base + 2 * t + 1:base + 2 * t + 2], op0=ALU.add, op1=ALU.add))
            return a, inverse_rms(a, 1, m)

        def square_x(t, x_ready):
            return join_halves([square_half(x_res[:, t, c * 512:(c + 1) * 512], x_ready[c], t, c, 0) for c in range(2)], t, 0)

        def scale_x(t, r):
            dve.wait(r[1])
            return [dve.step(partial(nc.vector.tensor_scalar, work_a[:, half_of(t, c)], x_res[:, t, c * 512:(c + 1) * 512],
                                     r[0], None, ALU.mult)) for c in range(2)]

        GROUPS = [[(0, 4), (4, 8)], [(0, 2), (2, 6), (6, 8)]]

        def turn_tile(t, normed):
            turned = []
            for g, (a, b) in enumerate(GROUPS[t]):
                if g < 2:
                    i = take_bank()
                else:
                    i = 7
                    pe.wait(*bank_free[i])
                    bank_free[i] = []
                for k in range(a, b):
                    pe.wait(ident_loaded, normed[k // 4])
                    at = t * D + k * P
                    issue = partial(nc.tensor.transpose, psum[i][:, (k - a) * P:(k - a + 1) * P], work_a[:, at:at + P], ident)
                    m = pe.step(issue) if k == b - 1 else pe.do(issue)
                turned.append((i, m))
            return turned

        def affine(t, g, turned, scale, shift, given):
            i, m = turned[g]
            a, b = GROUPS[t][g]
            act.wait(m, *given)
            full = {}
            for k in range(a, b):
                o, to = psum[i][:, (k - a) * P:(k - a + 1) * P], work_b[:, k, t * P:(t + 1) * P]
                if shift is None:
                    full[k] = act.step(partial(nc.scalar.activation, to, o, ACT.Copy, scale=scale[:, k:k + 1]))
                else:
                    full[k] = act.step(partial(nc.scalar.activation, to, o, ACT.Identity,
                                               scale=scale[:, k:k + 1], bias=shift[:, k:k + 1]))
            bank_free[i] = [full[k]]
            return full

        def split_h(t, a, b, full, ready):
            s, w = slice(a, b), slice(t * P, (t + 1) * P)
            dve.wait(full[b - 1], h_used[0])
            hi = dve.step(partial(nc.vector.tensor_copy, h_hi[:, s, w], work_b[:, s, w]))
            dve.wait(hi)
            lo = dve.step(partial(
                nc.vector.tensor_tensor, h_lo[:, s, w], work_b[:, s, w], h_hi[:, s, w].bitcast(F32), ALU.subtract))
            for k in range(a, b):
                ready[t, k] = (hi, lo)
            work_used[0] = lo

        def make_tile(t, normed, given, ready, between=None):
            turned = turn_tile(t, normed)
            pieces = [[(0, 2), (2, 4)], [(4, 8)]] if t == 0 else [[(0, 1), (1, 2)], [(2, 4), (4, 6)], [(6, 8)]]
            for g in range(len(turned)):
                full = affine(t, g, turned, *given)
                for a, b in pieces[g]:
                    split_h(t, a, b, full, ready)
                if g == 0 and between:
                    between()

        def of_tiles(ready):
            return lambda k, t=None: ready[t, k] if t is not None else [m for t in range(NT) for m in ready[t, k]]

        def gain_product(t, c, slot, ready):
            dve.wait(ready)
            m = dve.step(partial(nc.vector.tensor_tensor, work_a[:, half_of(t, c)],
                                 psum[4 + 2 * t + c][:, :], gain[slot][:, c * 512:(c + 1) * 512], ALU.mult))
            bank_free[4 + 2 * t + c] = [ready, m]
            return m

        def post_norm(marks, slot, then=None, tile_first=False):
            act.wait(work_used[0], work_v_used[0])
            dve.wait(work_used[0], gain_ready[slot])
            x_ready, normed, ready, r_x = [], [], {}, None
            for t in range(NT):
                squares = []
                for c in range(2):
                    squares.append(square_half(psum[4 + 2 * t + c][:, :], marks[t, c], t, c, 4))
                    if c == 0:
                        gained = gain_product(t, c, slot, squares[c])
                if r_x:
                    normed.append(scale_x(t - 1, r_x))
                a, r = join_halves(squares, t, 4)
                gained = gain_product(t, 1, slot, squares[1])
                dve.wait(r, gained)
                x_ready.append([dve.step(partial(
                    nc.vector.scalar_tensor_tensor, out=x_res[:, t, c * 512:(c + 1) * 512], in0=work_a[:, half_of(t, c)],
                    scalar=a, in1=x_res[:, t, c * 512:(c + 1) * 512], op0=ALU.mult, op1=ALU.add)) for c in range(2)])
                if t == NT - 1:
                    gain_used[slot] = gained
                    gain_ready[slot] = None
                    if then:
                        turned, given = turn_tile(0, normed[0]), then()
                        full = affine(0, 0, turned, *given)
                        split_h(0, 0, 2, full, ready)
                    evacuations = []
                    spare = [5, 7] if tile_first else [4, 5, 6]
                    while at_norm:
                        evacuations += at_norm.pop(0)(spare=spare)
                if then:
                    r_x = square_x(t, x_ready[t])
            if then:
                split_h(0, 2, 4, full, ready)
                normed.append(scale_x(NT - 1, r_x))
                full = affine(0, 1, turned, *given)
                if tile_first:
                    split_h(0, 4, KC, full, ready)
                    for evacuate in evacuations:
                        evacuate()
                    return of_tiles(ready), partial(make_tile, NT - 1, normed[-1], given, ready)
                make_tile(NT - 1, normed[-1], given, ready, partial(split_h, 0, 4, KC, full, ready))
            for evacuate in evacuations:
                evacuate()
            return of_tiles(ready) if then else x_ready

        h_of = (lambda k: h_hi[:, k, :], lambda k: h_lo[:, k, :])
        h_tok = (lambda k, t: h_hi[:, k, t * P:(t + 1) * P], lambda k, t: h_lo[:, k, t * P:(t + 1) * P])
        y_tok = (lambda k, t: y_hi[:, k, t * P:(t + 1) * P], lambda k, t: y_lo[:, k, t * P:(t + 1) * P])

        y_used = [None]

        def feed_forward(gate_up, down, base, ready, meanwhile={}):
            hidden_ready, hidden_used = {}, {}

            hidden = (lambda k, t: y_hi[:, k % 8, t * P:(t + 1) * P], lambda k, t: y_lo[:, k % 8, t * P:(t + 1) * P])

            def down_groups(*groups):
                m = weights_moving(down, [(base * FG + g, 2 * g, (0, 1)) for g in groups], *hidden,
                                   lambda k, t: hidden_ready[k // 2], 2, 2 * FG)
                for g in groups:
                    hidden_used[g] = m[NT - 1, 1]
                return m

            for g in range(FG):
                (gate,), gate_done = weights_still(gate_up, base * 2 * FG + g, *h_of, ready, KC, 2)
                s = slice(2 * (g % 4), 2 * (g % 4) + 2)
                tmp = work_v[:, g % 2, :].rearrange("p (a k n) -> p a k n", a=2, k=2)
                pair = lambda i: psum[i][:, :].rearrange("p (k n) -> p k n", k=2)
                act.wait(gate_done, work_v_used[0])
                silu = act.step(partial(nc.scalar.activation, tmp[:, 0], pair(gate), ACT.Silu))
                bank_free[gate] = [silu]
                (up,), up_done = weights_still(gate_up, base * 2 * FG + FG + g, *h_of, ready, KC, 2)
                dve.wait(silu, up_done)
                full = dve.step(partial(nc.vector.tensor_tensor, tmp[:, 1], pair(up), tmp[:, 0], ALU.mult))
                bank_free[up] = [full]
                act.wait(full, hidden_used.get(g - 4), y_used[0])
                hi = act.step(partial(nc.scalar.activation, y_hi[:, s, :], tmp[:, 1], ACT.Copy))
                dve.wait(hi, full)
                lo = dve.step(partial(nc.vector.tensor_tensor, 
                    y_lo[:, s, :], tmp[:, 1], y_hi[:, s, :].bitcast(F32), ALU.subtract))
                hidden_ready[g] = (hi, lo)
                if 0 < g < FG - 1:
                    down_groups(g - 1)
                if g in meanwhile:
                    meanwhile[g]()
            h_used[0] = up_done
            m = down_groups(FG - 2, FG - 1)
            y_used[0] = m[NT - 1, 1]
            work_v_used[0] = lo
            return m

        prob_turn, prob_t_turn = [0], [0]
        prob_free, prob_t_free = [None] * 4, [None] * 2
        W0, W1 = slice(0, P), slice(P, 3 * P)

        def exp_sum(b, top):
            z, s = prob[b], soft[:, b, :]
            act.wait(top)
            for t, w in enumerate((W0, W1)):
                ex = act.step(partial(nc.scalar.activation, z[:, w], z[:, w], ACT.Exp, bias=s[:, t:t + 1],
                                      accum_out=s[:, 2 + t:3 + t]))
            dve.wait(ex)
            return dve.step(partial(nc.vector.reciprocal, s[:, 4:6], s[:, 2:4]))

        def next_prob(score_done):
            b = prob_turn[0] % 4
            prob_turn[0] += 1
            dve.wait(score_done, prob_free[b])
            return b

        def decayed(i, score_done, h):
            b = next_prob(score_done)
            z, s = prob[b], soft[:, b, :]
            for t, w in enumerate((W0, W1)):
                last = dve.step(partial(
                    nc.vector.scalar_tensor_tensor, out=z[:, w], in0=psum[i][:, w], scalar=c_q[:, t * H + h:t * H + h + 1],
                    in1=mask[:, P:S] if t == 0 else mask, op0=ALU.add, op1=ALU.add))
            bank_free[i] = [last]
            dve.wait(last)
            for t, w in enumerate((W0, W1)):
                top = dve.step(partial(nc.vector.tensor_reduce, s[:, t:t + 1], z[:, w], AX_X, ALU.max, negate=True))
            return b, top

        def biased(i, score_done, head_bias):
            b = next_prob(score_done)
            z, s = prob[b], soft[:, b, :]
            for t, w in enumerate((W0, W1)):
                last = dve.step(partial(
                    nc.vector.tensor_tensor_reduce, out=z[:, w], in0=psum[i][:, w], in1=head_bias[:, P:S] if t == 0 else head_bias,
                    scale=1.0, scalar=-3e38, op0=ALU.add, op1=ALU.max, accum_out=s[:, 6 + t:7 + t]))
            bank_free[i] = [last]
            dve.wait(last)
            return b, dve.step(partial(nc.vector.tensor_scalar, s[:, 0:2], s[:, 6:8], -1.0, None, ALU.mult))

        def scale_prob(b, inv):
            z, s = prob[b], soft[:, b, :]
            dve.wait(inv)
            for t, w in enumerate((W0, W1)):
                last = dve.step(partial(nc.vector.tensor_scalar, z[:, w], z[:, w], s[:, 4 + t:5 + t], None, ALU.mult))
            return last

        def turn_psum(b, ready):
            z = prob[b]
            i = take_bank()
            pe.wait(ready)
            for c in range(3):
                issue = partial(nc.tensor.transpose, psum[i][:, c * P:(c + 1) * P], z[:, c * P:(c + 1) * P], ident)
                turned = pe.step(issue) if c == 2 else pe.do(issue)
            prob_free[b] = turned
            return i, turned

        def turn_prob(b, ready):
            i, turned = turn_psum(b, ready)
            u = prob_t_turn[0] % 2
            prob_t_turn[0] += 1
            act.wait(turned, prob_t_free[u])
            copied = act.step(partial(nc.scalar.activation, prob_t[u][:, :], psum[i][:, 0:3 * P], ACT.Copy))
            bank_free[i] = [copied]
            return u, copied

        def scores(q, k, more=None):
            i = take_bank()
            for t, w in enumerate((W0, W1)):
                o = psum[i][:, w]
                issue = partial(nc.tensor.matmul, 
                    o, q[:, t * P:(t + 1) * P], k[:, 0:(t + 1) * P], start=True, stop=more is None)
                if more is None:
                    m = pe.step(issue)
                else:
                    pe.do(issue)
                    m = more(i, t)
            return i, m

        def values_of(name, c, marks):
            for t in range(NT):
                act.wait(marks[t, c], work_v_used[0])
                i = 4 + 2 * t + c
                m = act.step(partial(nc.scalar.activation, work_v[:, t, c * 512:(c + 1) * 512], psum[i][:, :], ACT.Copy))
                bank_free[i] = [m]
                values_done[c].append(m)

        def token_values(name, c, ready, after, within=({}, {}), hold=(0, 0)):
            values_done[c] = []
            for half in range(2):
                marks = weights_moving(name, [(2 * c + half, half * KC // 2, (c,))], *h_tok, ready, KC // 2, KC,
                                       within[half], hold[half])
                if half:
                    values_of(name, c, marks)
                after[half]()

        def first_values_of(name, ready, second_tile):
            values_done[0] = []
            last = used[0] + 1

            def make_second():
                second_tile()
                split_up_to(last + AHEAD - 1)

            parts = [(half, half * KC // 2, (0,)) for half in range(2)]
            values_of(name, 0, weights_moving(name, parts, *h_tok, ready, KC // 2, KC, {(0, 0): make_second}, 1))

        values_done = {}

        act.wait(cols_loaded)
        c_ready = act.step(partial(nc.scalar.activation, c_act[:, :], col("c"), ACT.Silu))
        load_next()
        const_loaded = sync.dma(partial(nc.sync.dma_start, const[:, FLIP:], dram["const"][:, FLIP:]), const_in)
        wf_loaded = sync.dma(partial(nc.sync.dma_start, wf_raw[:, :], dram["wf"]), wf_in)
        for _ in range(N_RAW - 1):
            load_next()

        r_x = [square_x(t, [x_loaded[t]] * 2) for t in range(NT)]
        normed = [scale_x(t, r_x[t]) for t in range(NT)]
        done_items[0] = 1
        slab_split[0], _ = split_slab(0, 0, slice(0, SLAB // 2))
        second_half = []

        def split_second_half():
            marks, raw_free[0] = split_slab(0, 0, slice(SLAB // 2, SLAB))
            second_half.extend(marks)
            load_next()

        tiles = {}
        given = (col("mix_pre"), None, [cols_loaded])
        make_tile(0, normed[0], given, tiles, split_second_half)
        ready = of_tiles(tiles)
        act.wait(wf_loaded)
        wf_rounded = act.step(partial(nc.scalar.activation, wf_hi[:, :], wf_raw[:, :], ACT.Copy))
        dve.wait(wf_rounded)
        wf_rest = dve.step(partial(nc.vector.tensor_tensor, wf_lo[:, :], wf_raw[:, :], wf_hi[:, :].bitcast(F32), ALU.subtract))

        def forget_logits(n):
            if n == 0:
                gate_bank.append(take_bank())
                o = psum[gate_bank[0]][0:H, 0:S]
                pe.wait(wf_rest)
                for k in range(KC):
                    pe.wait(*ready(k))
                    vh, vl = wf_hi[:, k * H:(k + 1) * H], wf_lo[:, k * H:(k + 1) * H]
                    pe.do(partial(nc.tensor.matmul, o, vh, h_hi[:, k, :], start=k == 0, stop=False))
                    pe.do(partial(nc.tensor.matmul, o, vh, h_lo[:, k, :], start=False, stop=False))
                    m = pe.step(partial(nc.tensor.matmul, o, vl, h_hi[:, k, :], start=False, stop=k == KC - 1))
                dve.wait(m)
                gate_bank.append(dve.step(partial(nc.vector.tensor_copy, logits, o)))
            else:
                pe.wait(gate_bank[1])
                for t in range(NT):
                    m = pe.step(partial(nc.tensor.transpose, psum[gate_bank[0]][:, t * H:(t + 1) * H],
                                        logits[:, t * P:(t + 1) * P], ident[0:H, 0:H]))
                prob_free[3] = m
                gate_bank.append(m)

        gate_bank, logits = [], prob[3][0:H, 0:S]
        def make_second():
            make_tile(1, normed[1], given, tiles)
            split_up_to(AHEAD)

        values_done[0] = []
        weights_moving("v1", [(0, 0, (0,))], *h_tok, ready, KC // 2, KC, {(0, 0): make_second}, AHEAD)
        forget_logits(0)
        values_of("v1", 0, weights_moving("v1", [(1, KC // 2, (0,))], *h_tok, ready, KC // 2, KC))
        forget_logits(1)
        fb, _, f_done = gate_bank

        qT = work_b[:, 0:AC, :]
        kT = work_b[:, AC:2 * AC, :]
        qk_ready = {}
        heads1 = []

        def scores_first(h):
            q0 = (h % 2) * HD1
            part = slice(q0, q0 + HD1)
            pe.wait(*qk_ready[h // 4], *ck_ready)

            def minus_c(i, t):
                row = ident_r[:, h:h + 1].to_broadcast([H, P])
                o, w = psum[i][:, W1 if t else W0], slice(0, (t + 1) * P)
                pe.do(partial(nc.tensor.matmul, o, row, ck_hi[:, w], start=False, stop=False))
                return pe.step(partial(nc.tensor.matmul, o, row, ck_lo[:, w], start=False, stop=True))

            i, m = scores(qT[part, h // 2, :], kT[part, h // 2, :], minus_c)
            heads1.append((h, i, m))

        turned_first = []

        def finish_first():
            h, i, m = heads1.pop(0)
            dve.wait(cq_ready)
            b, top = decayed(i, m, h)
            behind_split.append(lambda: waiting.append((h, b, scale_prob(b, exp_sum(b, top)))))

        def turn_first(h, b, p_ready):
            turned_first.append((h, *turn_prob(b, p_ready)))

        def values_first(h, u, copied):
            rows = slice((h % 2) * HD1, (h % 2 + 1) * HD1)
            i = 4 + h // 2
            pe.wait(copied, *values_done[0], *bank_free[i])
            bank_free[i] = []
            o = psum[i]
            v = lambda c: work_v[:, c, h * HD1:(h + 1) * HD1]
            pe.do(partial(nc.tensor.matmul, o[rows, 0:S], v(0), prob_t[u][:, 0:S], start=True, stop=False))
            m = pe.step(partial(nc.tensor.matmul, o[rows, P:S], v(1), prob_t[u][:, S:3 * P], start=False, stop=True))
            prob_t_free[u] = m
            if h % 2 == 1:
                split_bank(i, o[:, 0:S], h // 2, m, y_used[0])
            return m

        y_ready = {}

        def split_bank(i, src, k, done, free, scale=None):
            act.wait(done, free)
            if scale is None:
                hi = act.step(partial(nc.scalar.activation, y_hi[:, k, :], src, ACT.Copy))
                dve.wait(hi, done)
                lo = dve.step(partial(nc.vector.tensor_tensor, y_lo[:, k, :], src, y_hi[:, k, :].bitcast(F32), ALU.subtract))
            else:
                hi = act.step(partial(nc.scalar.activation, y_hi[:, k, :], src, ACT.Copy, scale=scale))
                dve.wait(hi, done)
                lo = dve.step(partial(nc.vector.scalar_tensor_tensor, 
                    out=y_lo[:, k, :], in0=src, scalar=scale, in1=y_hi[:, k, :].bitcast(F32), op0=ALU.mult, op1=ALU.subtract))
            y_ready[k] = (hi, lo)
            bank_free[i] = [hi, lo]

        pair = lambda i: psum[i][:, :].rearrange("p (k n) -> p k n", k=2)
        waiting = []

        def attend_first(n):
            if 0 <= n - 3 < H:
                values_first(*turned_first.pop(0))
            if 0 <= n - 2 < H:
                turn_first(*waiting.pop(0))
            if n < H:
                scores_first(n)
                finish_first()

        def first_qk(g, keys):
            (i,), m = weights_still("qk1", 2 * keys + g, *h_of, ready, KC, 2)
            if keys:
                dve.wait(m)
                k = dve.step(partial(nc.vector.tensor_copy, kT[:, 2 * g:2 * g + 2, :], pair(i)))
            else:
                act.wait(m, *ready(KC - 1))
                k = act.step(partial(nc.scalar.activation, qT[:, 2 * g:2 * g + 2, :], pair(i), ACT.Copy, scale=HD1 ** -0.5))
            bank_free[i] = [k]
            qk_ready[g] = qk_ready.get(g, ()) + (k,)

        u, a, l, logf, nlogf = (gate_f[:, i, :] for i in range(5))
        dve.wait(f_done, cols_loaded)
        m = dve.step(partial(nc.vector.tensor_tensor, u, psum[fb][:, 0:NT * H], col("b_f"), ALU.add))
        bank_free[fb] = [m]
        act.wait(m)
        m = act.step(partial(nc.scalar.activation, a, u, ACT.Abs))
        act.wait(m)
        m = act.step(partial(nc.scalar.activation, a, a, ACT.Exp, scale=-1.0))
        dve.wait(m)
        m = dve.step(partial(nc.vector.tensor_scalar, a, a, 1.0, None, ALU.add))
        act.wait(m)
        m = act.step(partial(nc.scalar.activation, l, a, ACT.Ln))
        dve.wait(m)
        m = dve.step(partial(nc.vector.scalar_tensor_tensor, out=logf, in0=u, scalar=0.0, in1=l, op0=ALU.min, op1=ALU.subtract))
        dve.wait(m)
        logf_ready = dve.step(partial(nc.vector.tensor_scalar, nlogf, logf, -1.0, None, ALU.mult))

        l0 = COLUMNS["lam"][0]
        quarter = lambda n: cols[:, l0 + n * DIFF:l0 + (n + 1) * DIFF]
        for n in range(2):
            m = dve.step(partial(nc.vector.tensor_tensor, 
                lam_pr[:, n * DIFF:(n + 1) * DIFF], quarter(2 * n), quarter(2 * n + 1), ALU.mult))
        dve.wait(m)
        m = dve.step(partial(nc.vector.tensor_reduce, 
            lam_sb[:, 0:2], lam_pr[:, :].rearrange("p (a n) -> p a n", a=2), AX_X, ALU.add))
        act.wait(m)
        m = act.step(partial(nc.scalar.activation, lam_sb[:, 0:2], lam_sb[:, 0:2], ACT.Exp))
        dve.wait(m)
        m = dve.step(partial(nc.vector.scalar_tensor_tensor, 
            out=lam_sb[:, 2:3], in0=lam_sb[:, 0:1], scalar=LAMBDA_INIT, in1=lam_sb[:, 1:2], op0=ALU.add, op1=ALU.subtract))
        lam_ready = m
        dve.do(partial(nc.vector.tensor_scalar, subln_sc[:, :], col("subln"), 1.0 - LAMBDA_INIT, None, ALU.mult))

        first_qk(0, 0)
        first_qk(0, 1)
        cb = take_bank()
        pe.wait(logf_ready, const_loaded)
        for t in range(NT):
            o = psum[cb][:, t * H:(t + 1) * H]
            for c in range(t + 1):
                a, b = tri[:, (t - c) * P:(t - c + 1) * P], logf[:, c * H:(c + 1) * H]
                m = pe.step(partial(nc.tensor.matmul, o, a, b, start=c == 0, stop=c == t))
        o = psum[cb][0:H, S:2 * S]
        for c in range(NT):
            m = pe.step(partial(nc.tensor.matmul, o[:, c * P:S], nlogf[:, c * H:(c + 1) * H], tri[:, 0:S - c * P],
                                start=c == 0, stop=c == NT - 1))
        dve.wait(m)
        cq_ready = dve.step(partial(nc.vector.tensor_copy, c_q[:, :], psum[cb][:, 0:NT * H]))
        act.wait(cq_ready, ident_loaded)
        act.do(partial(nc.scalar.activation, ident_r[:, :], ident[0:H, 0:H], ACT.Copy))
        hi = act.step(partial(nc.scalar.activation, ck_hi[:, :], o, ACT.Copy))
        dve.wait(hi)
        lo = dve.step(partial(nc.vector.tensor_tensor, ck_lo[:, :], o, ck_hi[:, :].bitcast(F32), ALU.subtract))
        ck_ready = (hi, lo)
        bank_free[cb] = [lo]

        first_qk(1, 0)
        attend_first(0)
        first_qk(1, 1)
        attend_first(1)
        load_gain(0, dram["mix_post"][0])
        load_gain(1, dram["ffn_post"][0])
        load_gain(2, dram["norm_g"][0, 1])

        zc = bias[:, 0:AC, :]
        ya = bias[:, AC:2 * AC, :]
        conv_free = None
        for g in range(2):
            two = slice(2 * g, 2 * g + 2)
            (i,), m = weights_still("mix", 2 + g, *h_of, ready, KC, 2)
            act.wait(m)
            a = act.step(partial(nc.scalar.activation, zc[:, two, :], pair(i), ACT.Copy))
            bank_free[i] = [a]
            attend_first(2 * g + 2)
            (i,), m = weights_still("mix", 4 + g, *h_of, ready, KC, 2)
            dve.wait(m, a)
            z_ready = dve.step(partial(nc.vector.tensor_tensor, zc[:, two, :], pair(i), zc[:, two, :], ALU.mult))
            bank_free[i] = [z_ready]
            attend_first(2 * g + 3)
            for j in range(2 * g, 2 * g + 2):
                tap = lambda n, j=j: col("conv", 3 * j + n, 1)
                act.wait(z_ready)
                m = act.step(partial(nc.scalar.activation, ya[:, j, :], zc[:, j, :], ACT.Copy, scale=tap(2)))
                for shift in (1, 2):
                    dve.wait(m)
                    m = dve.step(partial(nc.vector.scalar_tensor_tensor, 
                        out=ya[:, j, shift:S], in0=zc[:, j, 0:S - shift], scalar=tap(2 - shift), in1=ya[:, j, shift:S],
                        op0=ALU.mult, op1=ALU.add))
        conv_done = m
        conv_ready = {}
        for g in range(2):
            two = slice(2 * g, 2 * g + 2)
            to = slice(AC + 2 * g, AC + 2 * g + 2)
            (i,), m = weights_still("mix", g, *h_of, ready, KC, 2)
            dve.wait(m, conv_done)
            full = dve.step(partial(nc.vector.tensor_tensor, ya[:, two, :], pair(i), ya[:, two, :], ALU.mult))
            bank_free[i] = [full]
            act.wait(full, y_used[0])
            hi = act.step(partial(nc.scalar.activation, y_hi[:, to, :], ya[:, two, :], ACT.Copy))
            dve.wait(hi, full)
            lo = dve.step(partial(nc.vector.tensor_tensor, 
                y_lo[:, to, :], ya[:, two, :], y_hi[:, to, :].bitcast(F32), ALU.subtract))
            conv_free = lo
            for k in (2 * g, 2 * g + 1):
                conv_ready[k] = (hi, lo)
            attend_first(6 + g)

        gate_c = work_a[:, :].rearrange("p (k n) -> p k n", k=KC)
        gate_a = bias
        gate_ready = {}
        for n, place in enumerate((gate_c, gate_a)):
            for g in range(4):
                (i,), m = weights_still("mix", 6 + 4 * n + g, *h_of, ready, KC, 2)
                act.wait(m, conv_free)
                s = act.step(partial(nc.scalar.activation, 
                    place[:, 2 * g:2 * g + 2, :], pair(i), ACT.Sigmoid))
                bank_free[i] = [s]
                gate_ready[n, g] = s
                if n == 0 and g < 3:
                    attend_first(H + g)
        h_used[0] = m

        conv_of = (lambda k: y_hi[:, AC + k, :], lambda k: y_lo[:, AC + k, :])
        attn_of = (lambda k: y_hi[:, k, :], lambda k: y_lo[:, k, :])
        merged = {}
        conv_part = {}
        for n in range(2):
            for half in range(2):
                src, rdy = (conv_of, lambda k: conv_ready[k]) if n == 0 else (attn_of, lambda k: y_ready[k])
                banks, m = weights_still("branch", 2 * n + half, *src, rdy, AC, 4)
                for b, i in enumerate(banks):
                    g = 2 * half + b
                    two = slice(2 * g, 2 * g + 2)
                    place = gate_c if n == 0 else gate_a
                    dve.wait(m, gate_ready[n, g])
                    full = dve.step(partial(nc.vector.tensor_tensor, 
                        place[:, two, :], pair(i), place[:, two, :], ALU.mult))
                    bank_free[i] = [full]
                    if n == 0:
                        conv_part[g] = full
                        continue
                    dve.wait(full, conv_part[g])
                    full = dve.step(partial(nc.vector.tensor_tensor, 
                        gate_a[:, two, :], gate_a[:, two, :], gate_c[:, two, :], ALU.add))
                    act.wait(full, h_used[0])
                    hi = act.step(partial(nc.scalar.activation, h_hi[:, two, :], gate_a[:, two, :], ACT.Copy))
                    dve.wait(hi, full)
                    lo = dve.step(partial(nc.vector.tensor_tensor, 
                        h_lo[:, two, :], gate_a[:, two, :], h_hi[:, two, :].bitcast(F32), ALU.subtract))
                    for k in (2 * g, 2 * g + 1):
                        merged[k] = (hi, lo)
        y_used[0] = m
        work_used[0] = full
        work_v_used[0] = m

        def wide_product(name, order, tok, rdy, extra={}, hold=0):
            part = lambda index: (index, index % 2 * KC // 2, (index // 2,))
            for n, index in enumerate(order[:2]):
                weights_moving(name, [part(index)], *tok, rdy, KC // 2, KC,
                               {(t, 0): extra[n, t] for t in range(NT) if (n, t) in extra}, n * hold)
            return weights_moving(name, [part(index) for index in order[2:]], *tok, rdy, KC // 2, KC, {}, hold)

        marks = wide_product("out1", (0, 2, 1, 3), h_tok, lambda k, t: merged[k])
        h_used[0] = marks[NT - 1, 1]
        ready = post_norm(marks, 0, lambda: (col("ffn_pre"), None, []))
        load_gain(0, dram["norm_g"][0, 3])

        table, hot = prob[0][0:BUCKETS + 1, 0:H], prob[1][0:BUCKETS + 1, :]
        bias_ready, diagonal_in = [], []
        bias_given = [prob_free[0], prob_free[1], work_used[0]]

        def load_table():
            pool.wait(*bias_given)
            pool.dma(partial(nc.gpsimd.dma_start, table, dram["rel_table"]), table_in)
            bias_given.append(pool.dma(partial(nc.gpsimd.dma_start, hot, dram["bucket_of"]), table_in))

        def spread_table():
            i = take_bank()
            pe.wait(bias_given[-1])
            m = pe.step(partial(nc.tensor.matmul, psum[i][0:H, 0:BIAS_W], table, hot, start=True, stop=True))
            dve.wait(m, prob_free[2])
            rows = dve.step(partial(nc.vector.tensor_copy, prob[2][0:H, :], psum[i][0:H, 0:BIAS_W]))
            bank_free[i] = [rows]
            pool.wait(rows)
            kept = pool.dma(partial(nc.gpsimd.dma_start, bias_dram, prob[2][0:H, :]), bias_sig)
            pool.wait(kept)
            diagonal = bass.AP(bias_dram.tensor, 0, [[1, P], [BIAS_W, H], [1, S]])
            diagonal_in.append(pool.dma(partial(nc.gpsimd.dma_start, bias[:, :, :], diagonal), bias_sig))
            prob_free[0] = prob_free[1] = m
            prob_free[2] = kept

        def flip_bias():
            pe.wait(diagonal_in[0])
            for h in range(0, H, 2):
                i = take_bank()
                two = bias[:, h:h + 2, :]
                flipped = pe.step(partial(nc.tensor.matmul, pair(i), flip, two, start=True, stop=True))
                dve.wait(flipped)
                bias_ready.append(dve.step(partial(nc.vector.tensor_copy, two, pair(i))))
                bank_free[i] = [bias_ready[-1]]

        marks = feed_forward("gate_up1", "down1", 0, ready, {0: load_table, 2: spread_table, 5: flip_bias})
        def modulation(layer, part):
            at = 4 * layer + 2 * part
            return mod_cols[:, at, :], mod_cols[:, at + 1, :], [mod_ready[layer, part, 0], mod_ready[layer, part, 1]]

        ready, second_tile = post_norm(marks, 1, partial(modulation, 0, 0), tile_first=True)
        load_gain(1, dram["norm_g"][1, 1])

        for layer, name in enumerate(("moba", "diff")):
            q_scale = (HD2 if layer == 0 else DIFF) ** -0.5
            heads = work[:, :].rearrange("p (h n) -> p h n", h=H)
            qk_ready, softened, turned_heads, diff_squares = {}, {}, {}, {}
            y_ready.clear()

            def score_head(h):
                pe.wait(*qk_ready[h // 2])
                halves = 1 if layer == 0 else 2
                width = P // halves
                got = []
                for c in range(halves):
                    part = slice(c * width, (c + 1) * width)
                    i, m = scores(heads[part, h, 0:S], heads[part, h, S:2 * S])
                    dve.wait(bias_ready[-1])
                    got.append(biased(i, m, bias[:, h, :]))
                behind_split.append(partial(finish_head, h, got))

            def finish_head(h, got):
                got = [(b, exp_sum(b, top)) for b, top in got]
                b, inv = got[0]
                last = scale_prob(b, inv)
                if layer == 1:
                    b2, inv2 = got[1]
                    s2 = soft[:, b2, :]
                    dve.wait(inv2, lam_ready)
                    m2 = dve.step(partial(nc.vector.tensor_scalar, s2[:, 4:6], s2[:, 4:6], lam_sb[:, 2:3], -1.0, ALU.mult, ALU.mult))
                    dve.wait(m2, last)
                    for t, w in enumerate((W0, W1)):
                        last = dve.step(partial(
                            nc.vector.scalar_tensor_tensor, out=prob[b][:, w], in0=prob[b2][:, w],
                            scalar=s2[:, 4 + t:5 + t], in1=prob[b][:, w], op0=ALU.mult, op1=ALU.add))
                    prob_free[b2] = last
                softened[h] = (b, last)

            def turn_head(h):
                b, p_ready = softened[h]
                i, turned = turn_psum(b, p_ready)
                act.wait(turned)
                copied = act.step(partial(nc.scalar.activation, heads[:, h, 0:3 * P], psum[i][:, 0:3 * P], ACT.Copy))
                bank_free[i] = [copied]
                turned_heads[h] = copied

            def apply_two_heads(h, i):
                pe.wait(turned_heads[h + 1], *values_done[h // 4], *bank_free[i])
                for a in range(2):
                    v = lambda c: work_v[:, c, (h + a) * P:(h + a + 1) * P]
                    o, pt = psum[i][:, a * S:(a + 1) * S], heads[:, h + a, :]
                    pe.do(partial(nc.tensor.matmul, o[:, 0:P], pt[:, 0:P], v(0), start=True, stop=True))
                    pe.do(partial(nc.tensor.matmul, o[:, P:S], pt[:, P:S], v(0), start=True, stop=False))
                    m = pe.step(partial(nc.tensor.matmul, o[:, P:S], pt[:, S:3 * P], v(1), start=False, stop=True))
                dve.wait(m)
                o_copied = dve.step(partial(nc.vector.tensor_copy, heads[:, h:h + 2, 0:S], pair(i)))
                bank_free[i] = [o_copied]
                act.wait(o_copied)
                for a in range(2 * NT):
                    act.wait(square_free[0])
                    square_free[0] = act.step(partial(
                        nc.scalar.activation, lam_pr[:, :], heads[:, h + a // NT, a % NT * P:(a % NT + 1) * P], ACT.Square,
                        accum_out=diff_stat[:, NT * h + a:NT * h + a + 1]))
                diff_squares[h + 1] = square_free[0]
                return m

            def apply_head(h):
                i = take_bank()
                pe.wait(turned_heads[h], *values_done[h // 4])
                v = lambda c: work_v[:, c, h * P:(h + 1) * P]
                o, pt = psum[i], heads[:, h, :]
                pe.do(partial(nc.tensor.matmul, o[:, 0:S], v(0), pt[:, 0:S], start=True, stop=False))
                m = pe.step(partial(nc.tensor.matmul, o[:, P:S], v(1), pt[:, S:3 * P], start=False, stop=True))
                split_bank(i, o[:, 0:S], h, m, y_used[0])
                return m

            square_free = [lam_ready]

            def head_rms(hs):
                n = NT * len(hs)
                sums = diff_stat[:, NT * hs[0]:NT * hs[0] + n]
                dve.wait(diff_squares[hs[-1]])
                m = dve.step(partial(nc.vector.tensor_scalar, sums, sums, 1.0 / HD2, EPS, ALU.mult, ALU.add))
                return inverse_rms(sums, n, m)

            def scale_heads(hs, r):
                dve.wait(r)
                scaled = {}
                for h in hs:
                    for t in range(NT):
                        w = heads[:, h, t * P:(t + 1) * P]
                        scaled[h] = dve.step(partial(
                            nc.vector.tensor_scalar, w, w, diff_stat[:, NT * h + t:NT * h + t + 1], None, ALU.mult))
                return scaled

            def turn_heads(hs, scaled):
                for h in hs:
                    i = take_bank()
                    pe.wait(scaled[h])
                    for t in range(NT):
                        m = pe.step(partial(nc.tensor.transpose, psum[i][:, t * P:(t + 1) * P], heads[:, h, t * P:(t + 1) * P], ident))
                    split_bank(i, psum[i][:, 0:S], h, m, y_used[0], scale=subln_sc[:, 0:1])
                return m

            def attend(n):
                if layer == 0 and 0 <= n - 3 < 4:
                    apply_head(n - 3)
                if 0 <= n - 2 < H:
                    turn_head(n - 2)
                if 0 <= n < H:
                    score_head(n)

            if layer == 0:
                first_values_of(name + "_v", ready, second_tile)
            for g in range(4):
                two = slice(2 * g, 2 * g + 2)
                (i,), m = weights_still(name + "_qk", g, *h_of, ready, KC, 2)
                act.wait(m, work_used[0])
                q = act.step(partial(nc.scalar.activation, heads[:, two, 0:S], pair(i), ACT.Copy, scale=q_scale))
                bank_free[i] = [q]
                attend(2 * g - 2)
                (i,), m = weights_still(name + "_qk", 4 + g, *h_of, ready, KC, 2)
                act.wait(m)
                k = act.step(partial(nc.scalar.activation, heads[:, two, S:2 * S], pair(i), ACT.Copy))
                bank_free[i] = [k]
                qk_ready[g] = (q, k)
                attend(2 * g - 1)

            last_read = [None]
            if layer == 0:
                token_values(name + "_v", 1, ready, [partial(attend, 6), partial(attend, 7)])

                def late_turns():
                    turn_head(6)
                    apply_head(4)
                    apply_head(5)
                    turn_head(7)

                def late_values():
                    apply_head(6)
                    last_read[0] = apply_head(7)

                extra = {(0, 1): late_turns, (1, 0): late_values}
            else:
                scaled = {}

                def apply_pairs(*pairs):
                    for h, i in pairs:
                        apply_two_heads(h, take_bank() if i is None else i)
                        scaled[h] = head_rms(range(h, h + 2))

                def scale_pairs(*pairs):
                    for h in pairs:
                        scaled[h] = scale_heads(range(h, h + 2), scaled[h])

                def turn_pairs(*pairs):
                    for h in pairs:
                        last_read[0] = turn_heads(range(h, h + 2), scaled[h])

                def early_values():
                    apply_pairs((0, 4), (2, 6))

                def early_scales():
                    attend(8)
                    scale_pairs(0, 2)

                def early_turns():
                    turn_pairs(2)
                    attend(9)

                token_values(name + "_v", 0, ready, [partial(attend, 6), partial(attend, 7)])
                token_values(name + "_v", 1, ready, [early_scales, early_turns],
                             [{(0, 0): early_values}, {(0, 0): partial(turn_pairs, 0)}], (0, 1))

                def late_pair():
                    apply_pairs((6, None))
                    scale_pairs(4, 6)

                extra = {(0, 0): partial(apply_pairs, (4, None)), (0, 1): late_pair, (1, 1): partial(turn_pairs, 4, 6)}
            h_used[0] = values_done[1][-1]
            marks = wide_product(name + "_o", (0, 2, 1, 3), y_tok, lambda k, t: y_ready[k], extra, layer)
            work_v_used[0] = work_used[0] = last_read[0]
            y_used[0] = marks[NT - 1, 1]
            slot = gain_slot[layer, 0]
            ready = post_norm(marks, slot, partial(modulation, layer, 1))
            if layer == 0:
                load_gain(slot, dram["norm_g"][1, 3])
            marks = feed_forward("gate_up2", "down2", layer, ready)
            ready = post_norm(marks, gain_slot[layer, 1], partial(modulation, layer + 1, 0) if layer == 0 else None)

        for t in range(NT):
            for c in range(2):
                sync.wait(ready[t][c])
                s = slice(c * 512, (c + 1) * 512)
                done = sync.dma(partial(nc.sync.dma_start, out[t * P:(t + 1) * P, s], x_res[:, t, s]), stored)
        sync.wait(done)

        block = ctx.enter_context(nc.Block())

        @block.sync
        def _(e):
            sync.play(e)

        @block.scalar
        def _(e):
            act.play(e)

        @block.vector
        def _(e):
            dve.play(e)

        @block.gpsimd
        def _(e):
            pool.play(e)

        @block.tensor
        def _(e):
            pe.play(e)


def kernel(**inputs):
    import numpy as np
    import concourse.bacc as bacc
    from concourse.bass_utils import run_bass_kernel_spmd as run

    a = {name: np.asarray(value) for name, value in inputs.items()}
    put = np.ascontiguousarray

    def slabs(w, kcs, width):
        K, N = w.shape
        return put(w.reshape(K // (P * kcs), kcs, P, N // width, width).transpose(3, 0, 2, 1, 4)).reshape(-1, P, kcs * width)

    def columns(v):
        return v.reshape(-1, P).T

    w_in = a["w_in"][0]
    rest = 3 * AW + H
    qkv = {"moba": a["moba_w_qkv_2"][0], "diff": a["diff_w_qkv_2"][0]}
    rel = (BIAS_W - P - 1) - np.arange(BIAS_W)
    n = np.maximum(rel, 1).astype(np.float32)
    half = BUCKETS // 2
    far = half + (np.log(n / half) / math.log(2048 / half) * (BUCKETS - half)).astype(np.int32)
    bucket = np.where(rel < half, rel, np.minimum(far, BUCKETS - 1))
    bucket = np.where(rel < 0, BUCKETS, bucket)
    bucket_of = (bucket[None, :] == np.arange(BUCKETS + 1)[:, None]).astype(np.float32)
    const = np.zeros((P, N_CONST), np.float32)
    row, s = np.arange(P)[:, None], np.arange(S)[None, :]
    const[:, IDENT:IDENT + P] = np.eye(P)
    const[:, ONES:ONES + P] = 1.0
    const[:, FLIP:FLIP + P] = np.eye(P)[::-1]
    const[:, TRI:TRI + P] = row <= s[:, 0:P]
    const[:, MASK:MASK + S] = np.where(s > row + P, NEG, 0.0)
    small = {
        "mix_pre": columns(a["norm_mix_pre"][0]), "ffn_pre": columns(a["norm_ffn_pre"][0]), "c": columns(a["c_2"][0]),
        "g00": columns(a["norm_g_2"][0, 0]), "g02": columns(a["norm_g_2"][0, 2]),
        "g10": columns(a["norm_g_2"][1, 0]), "g12": columns(a["norm_g_2"][1, 2]),
        "conv": a["conv_w"][0].reshape(3, AC, P).transpose(2, 1, 0).reshape(P, 3 * AC),
        "subln": columns(a["diff_subln_g_2"][0]),
        "b_f": np.broadcast_to(np.concatenate([a["b_f"][0]] * NT)[None, :], (P, NT * H)),
        "lam": np.broadcast_to(a["diff_lambda_2"][0].reshape(1, -1), (P, 4 * DIFF)),
    }
    arrays = {
        "x": a["x"][0],
        "cols": np.concatenate([small[k] for k in COLUMNS], axis=1),
        "const": const,
        "bucket_of": bucket_of,
        "rel_table": np.concatenate([a["rel_bias_2"], np.full((1, H), NEG, np.float32)], axis=0),
        "wf": w_in[:, 3 * AW:rest].reshape(KC, P, H).transpose(1, 0, 2).reshape(P, KC * H),
        "qk1": slabs(w_in[:, 0:2 * AW], KC, 256),
        "v1": slabs(w_in[:, 2 * AW:3 * AW], KC // 2, 512),
        "mix": slabs(w_in[:, rest:], KC, 256),
        "branch": np.concatenate([slabs(a["w_branch"][0, i], AC, 512) for i in range(2)]),
        "out1": slabs(a["w_out"][0], KC // 2, 512),
        "gate_up1": slabs(a["w_gate_up"][0], KC, 256),
        "down1": slabs(a["w_down"][0], 2, D),
        "gate_up2": np.concatenate([slabs(a["ffn_w_in_2"][i], KC, 256) for i in range(2)]),
        "down2": np.concatenate([slabs(a["ffn_w_out_2"][i], 2, D) for i in range(2)]),
        "ada": np.concatenate([slabs(a["ada_w_2"][i], 1, SLAB) for i in range(2)]),
        "ada_b": a["ada_b_2"].reshape(-1, SLAB),
        "mix_post": a["norm_mix_post"], "ffn_post": a["norm_ffn_post"], "norm_g": a["norm_g_2"],
    }
    for name, w in qkv.items():
        arrays[name + "_qk"] = slabs(w[:, 0:2 * D], KC, 256)
        arrays[name + "_v"] = slabs(w[:, 2 * D:], KC // 2, 512)
        arrays[name + "_o"] = slabs(a[name + "_w_o_2"][0], KC // 2, 512)

    nc = bacc.Bacc("TRN2", target_bir_lowering=False, num_devices=1, dynamic_dma_scratch_size=2048)
    arrays = {"in_" + k: put(v) for k, v in arrays.items()}
    dram = {k[3:]: nc.dram_tensor(k, v.shape, mybir.dt.from_np(v.dtype), kind="ExternalInput").ap() for k, v in arrays.items()}
    out = nc.dram_tensor("out", (S, D), F32, kind="ExternalOutput").ap()
    build_program(nc, dram, out)
    result = run(nc, [arrays], core_ids=[0])
    return result.results[0]["out"].reshape(1, S, D)
```
